# Optimizing a Trainium2 kernel written in Bass

```python
import math
import jax, jax.numpy as jnp
from jax import lax
import numpy as np

D_MODEL = 1024
BATCH = 1
SEQ = 1024
DEPTH = 1
DEC_BATCH = 8
DEC_SEQ = 8
PAST_LEN = 2048
PAGE_SIZE = 128

MIX_A = 512
A_GROUPS = 4
A_GW = MIX_A // A_GROUPS
CHUNK = 128
N_HEADS = 8
N_KV = 2
HEAD_DIM = 64
GQA = N_HEADS // N_KV
MIX_B = N_HEADS * HEAD_DIM
WINDOW = 128
IN_COLS = 2 * MIX_A + (N_HEADS + 2 * N_KV) * HEAD_DIM
REL_BUCKETS = 32
REL_MAX_EXACT = REL_BUCKETS // 2
REL_MAX_DIST = 128
N_MEM = 256
MEM_HEADS = 4
MEM_HEAD_DIM = 128
MEM_INNER = MEM_HEADS * MEM_HEAD_DIM
PEER_HEADS = 8
PEER_KEYS = 128
PEER_N = PEER_KEYS * PEER_KEYS
PEER_HALF = 128
PEER_QDIM = 2 * PEER_HALF
PEER_TOPK = 16
PEER_BLOCK = 128
EPS = 1e-6

kernel_name = 'hymba_gmlp_swa_peer_step'

def rms_norm(x, g):
    xf = x.astype(jnp.float32)
    y = xf * lax.rsqrt(jnp.mean(xf * xf, axis=-1, keepdims=True) + EPS)
    return (y * g.astype(jnp.float32)).astype(x.dtype)

def layer_norm_groups(v, g, b):
    vf = v.astype(jnp.float32).reshape(v.shape[:-1] + (A_GROUPS, A_GW))
    mu = jnp.mean(vf, axis=-1, keepdims=True)
    var = jnp.mean(jnp.square(vf - mu), axis=-1, keepdims=True)
    y = (vf - mu) * lax.rsqrt(var + EPS)
    y = y * g.astype(jnp.float32).reshape(A_GROUPS, A_GW) + b.astype(jnp.float32).reshape(A_GROUPS, A_GW)
    return y.astype(v.dtype)

def t5_bucket(d):
    n = jnp.maximum(d, 0)
    nf = jnp.maximum(n, 1).astype(jnp.float32)
    large = REL_MAX_EXACT + (jnp.log(nf / REL_MAX_EXACT) / math.log(REL_MAX_DIST / REL_MAX_EXACT)
                             * (REL_BUCKETS - REL_MAX_EXACT)).astype(jnp.int32)
    large = jnp.minimum(large, REL_BUCKETS - 1)
    return jnp.where(n < REL_MAX_EXACT, n, large)

def rel_bias_logits(d, rel_bias):
    b = rel_bias[t5_bucket(d)]
    return jnp.moveaxis(b, -1, 0).reshape((N_KV, GQA) + d.shape).astype(jnp.float32)

def attend_sink(q, k, v, bias, mask, sink):
    s = jnp.einsum('...qkgd,...skd->...kgqs', q, k).astype(jnp.float32) / math.sqrt(HEAD_DIM) + bias
    s = jnp.where(mask, s, -1e30)
    sk = sink.astype(jnp.float32).reshape(N_KV, GQA, 1, 1)
    m = jnp.maximum(jnp.max(s, axis=-1, keepdims=True), sk)
    p = jnp.exp(s - m)
    p = p / (jnp.sum(p, axis=-1, keepdims=True) + jnp.exp(sk - m))
    return jnp.einsum('...kgqs,...skd->...qkgd', p.astype(v.dtype), v)

def mix_inputs(x, norm_g, w_in, ln_g, ln_b):
    xn = rms_norm(x, norm_g)
    h = xn @ w_in
    z = jax.nn.gelu(h[..., :2 * MIX_A])
    u = z[..., :MIX_A]
    v = layer_norm_groups(z[..., MIX_A:], ln_g, ln_b)
    r = h[..., 2 * MIX_A:]
    lead = x.shape[:-1]
    q = r[..., :MIX_B]
    k = r[..., MIX_B:MIX_B + N_KV * HEAD_DIM].reshape(lead + (N_KV, HEAD_DIM))
    vb = r[..., MIX_B + N_KV * HEAD_DIM:].reshape(lead + (N_KV, HEAD_DIM))
    return u, v, q, k, vb

def spatial_gate_prompt(v, w_s, b_s):
    B, S = v.shape[:2]
    vc = v.reshape(B, S // CHUNK, CHUNK, A_GROUPS, A_GW)
    wm = w_s * jnp.tril(jnp.ones((CHUNK, CHUNK), w_s.dtype))
    out = jnp.einsum('gts,bcsgd->bctgd', wm, vc) + b_s.T[None, None, :, :, None]
    return out.reshape(B, S, A_GROUPS, A_GW)

def spatial_gate_sample(v, w_s, b_s):
    L = v.shape[1]
    wm = (w_s * jnp.tril(jnp.ones((CHUNK, CHUNK), w_s.dtype)))[:, :L, :L]
    return jnp.einsum('gts,bsgd->btgd', wm, v) + b_s[:, :L].T[None, :, :, None]

def swa_prompt(q, k, v, rel_bias, sink):
    B, S = q.shape[:2]
    nb = S // WINDOW
    qb = q.reshape(B, nb, WINDOW, N_KV, GQA, HEAD_DIM)
    kb = k.reshape(B, nb, WINDOW, N_KV, HEAD_DIM)
    vb = v.reshape(B, nb, WINDOW, N_KV, HEAD_DIM)
    padw = ((0, 0), (1, 0), (0, 0), (0, 0), (0, 0))
    kk = jnp.concatenate([jnp.pad(kb[:, :-1], padw), kb], axis=2)
    vv = jnp.concatenate([jnp.pad(vb[:, :-1], padw), vb], axis=2)
    qi = jnp.arange(WINDOW)[:, None] + WINDOW
    kj = jnp.arange(2 * WINDOW)[None, :]
    d = qi - kj
    band = (d >= 0) & (d < WINDOW)
    mask = band[None] & ((jnp.arange(nb)[:, None, None] > 0) | (kj[None] >= WINDOW))
    o = attend_sink(qb, kk, vv, rel_bias_logits(d, rel_bias), mask[None, :, None, None], sink)
    return o.reshape(B, S, MIX_B)

def swa_sample(q, k_new, v_new, k_buf, v_buf, rel_bias, sink):
    N, L = q.shape[:2]
    wb = k_buf.shape[1]
    kk = jnp.concatenate([k_buf, k_new], axis=1)
    vv = jnp.concatenate([v_buf, v_new], axis=1)
    d = (wb + jnp.arange(L))[:, None] - jnp.arange(wb + L)[None, :]
    mask = (d >= 0) & (d < WINDOW)
    qh = q.reshape(N, L, N_KV, GQA, HEAD_DIM)
    o = attend_sink(qh, kk, vv, rel_bias_logits(d, rel_bias), mask, sink)
    return o.reshape(N, L, MIX_B), kk[:, -wb:], vv[:, -wb:]

def mix_outputs(x, u, s, o_b, g_a, g_b, w_out):
    y_a = u * s.reshape(u.shape)
    y = jnp.concatenate([rms_norm(y_a, g_a), rms_norm(o_b, g_b)], axis=-1) @ w_out
    return x + y

def memory_kv(mem, g_src, w_mk, w_mv):
    N, M = mem.shape[:2]
    mn = rms_norm(mem, g_src)
    mk = (mn @ w_mk).reshape(N, M, MEM_HEADS, MEM_HEAD_DIM)
    mv = (mn @ w_mv).reshape(N, M, MEM_HEADS, MEM_HEAD_DIM)
    return mk, mv

def memory_attn(x, g, w_mq, w_mo, mk, mv):
    N, L = x.shape[:2]
    q = (rms_norm(x, g) @ w_mq).reshape(N, L, MEM_HEADS, MEM_HEAD_DIM)
    s = jnp.einsum('nlhd,nmhd->nhlm', q, mk).astype(jnp.float32) / math.sqrt(MEM_HEAD_DIM)
    p = jax.nn.softmax(s, axis=-1).astype(mv.dtype)
    o = jnp.einsum('nhlm,nmhd->nlhd', p, mv).reshape(N, L, MEM_INNER)
    return x + o @ w_mo

def peer_ffn(x, g, w_q, keys, e_u, e_v):
    N, L, D = x.shape
    xn = rms_norm(x, g).reshape(N * L, D)
    T = N * L
    nblk = -(-T // PEER_BLOCK)
    xb = jnp.pad(xn, ((0, nblk * PEER_BLOCK - T), (0, 0))).reshape(nblk, PEER_BLOCK, D)

    def one_block(xt):
        q = (xt @ w_q).reshape(PEER_BLOCK, PEER_HEADS, 2, PEER_HALF)
        s = jnp.einsum('thpc,hpnc->thpn', q, keys).astype(jnp.float32)
        s1, i1 = lax.top_k(s[:, :, 0], PEER_TOPK)
        s2, i2 = lax.top_k(s[:, :, 1], PEER_TOPK)
        cand = (s1[..., :, None] + s2[..., None, :]).reshape(PEER_BLOCK, PEER_HEADS, PEER_TOPK * PEER_TOPK)
        cidx = (i1[..., :, None] * PEER_KEYS + i2[..., None, :]).reshape(PEER_BLOCK, PEER_HEADS, PEER_TOPK * PEER_TOPK)
        sc, pos = lax.top_k(cand, PEER_TOPK)
        eidx = jnp.take_along_axis(cidx, pos, axis=-1)
        gate = jax.nn.softmax(sc, axis=-1)
        act = jax.nn.gelu(jnp.einsum('thkd,td->thk', e_u[eidx], xt).astype(jnp.float32))
        w = (gate * act).astype(xt.dtype)
        return jnp.einsum('thk,thkd->td', w, e_v[eidx])

    out = lax.map(one_block, xb).reshape(nblk * PEER_BLOCK, D)[:T].reshape(N, L, D)
    return x + out

def setup_inputs(seed: int = 0) -> dict:
    key = jax.random.key(seed)
    ks = jax.random.split(key, 32)
    f32 = jnp.float32

    def nrm(k, shape, scale):
        return jax.random.normal(k, shape, f32) * scale

    def gain(k, shape):
        return 1.0 + 0.01 * jax.random.normal(k, shape, f32)

    w_buf = min(WINDOW, PAST_LEN)
    D = D_MODEL
    return {
        'x_prompt': nrm(ks[0], (BATCH, SEQ, D), 1.0),
        'x_sample': nrm(ks[1], (DEC_BATCH, DEC_SEQ, D), 1.0),
        'mem_prompt': nrm(ks[2], (BATCH, N_MEM, D), 1.0),
        'cache_swa_k': nrm(ks[3], (DEPTH, DEC_BATCH, w_buf, N_KV, HEAD_DIM), 1.0),
        'cache_swa_v': nrm(ks[4], (DEPTH, DEC_BATCH, w_buf, N_KV, HEAD_DIM), 1.0),
        'cache_mem_k': nrm(ks[5], (DEPTH, DEC_BATCH, N_MEM, MEM_HEADS, MEM_HEAD_DIM), 1.0),
        'cache_mem_v': nrm(ks[6], (DEPTH, DEC_BATCH, N_MEM, MEM_HEADS, MEM_HEAD_DIM), 1.0),
        'norm_mix_g': gain(ks[7], (DEPTH, D)),
        'w_in': nrm(ks[8], (DEPTH, D, IN_COLS), D ** -0.5),
        'ln_v_g': gain(ks[9], (DEPTH, MIX_A)),
        'ln_v_b': nrm(ks[10], (DEPTH, MIX_A), 0.01),
        'spatial_w': nrm(ks[11], (DEPTH, A_GROUPS, CHUNK, CHUNK), CHUNK ** -0.5),
        'spatial_b': gain(ks[12], (DEPTH, A_GROUPS, CHUNK)),
        'attn_sinks': nrm(ks[13], (DEPTH, N_HEADS), 0.5),
        'rel_bias': nrm(ks[14], (REL_BUCKETS, N_HEADS), 0.5),
        'norm_a_out_g': gain(ks[15], (DEPTH, MIX_A)),
        'norm_b_out_g': gain(ks[16], (DEPTH, MIX_B)),
        'w_out': nrm(ks[17], (DEPTH, MIX_A + MIX_B, D), (MIX_A + MIX_B) ** -0.5),
        'norm_mem_g': gain(ks[18], (DEPTH, D)),
        'norm_memsrc_g': gain(ks[19], (DEPTH, D)),
        'w_mq': nrm(ks[20], (DEPTH, D, MEM_INNER), D ** -0.5),
        'w_mk': nrm(ks[21], (DEPTH, D, MEM_INNER), D ** -0.5),
        'w_mv': nrm(ks[22], (DEPTH, D, MEM_INNER), D ** -0.5),
        'w_mo': nrm(ks[23], (DEPTH, MEM_INNER, D), MEM_INNER ** -0.5),
        'norm_ffn_g': gain(ks[24], (DEPTH, D)),
        'peer_wq': nrm(ks[25], (DEPTH, D, PEER_HEADS * PEER_QDIM), D ** -0.5),
        'peer_keys': nrm(ks[26], (DEPTH, PEER_HEADS, 2, PEER_KEYS, PEER_HALF), PEER_HALF ** -0.5),
        'peer_u': nrm(ks[27], (DEPTH, PEER_N, D), D ** -0.5),
        'peer_v': nrm(ks[28], (DEPTH, PEER_N, D), PEER_HEADS ** -0.5),
        'norm_final_g': gain(ks[29], (D,)),
    }

def reference(x_prompt, x_sample, mem_prompt, cache_swa_k, cache_swa_v, cache_mem_k, cache_mem_v,
              norm_mix_g, w_in, ln_v_g, ln_v_b, spatial_w, spatial_b, attn_sinks, rel_bias,
              norm_a_out_g, norm_b_out_g, w_out, norm_mem_g, norm_memsrc_g, w_mq, w_mk, w_mv, w_mo,
              norm_ffn_g, peer_wq, peer_keys, peer_u, peer_v, norm_final_g):
    hp, hs = x_prompt, x_sample
    swa_k_p, swa_v_p, mem_k_p, mem_v_p = [], [], [], []
    swa_k_s, swa_v_s, chunk_v_s = [], [], []
    for l in range(DEPTH):
        u, v, q, k, vb = mix_inputs(hp, norm_mix_g[l], w_in[l], ln_v_g[l], ln_v_b[l])
        s_gate = spatial_gate_prompt(v, spatial_w[l], spatial_b[l])
        o_b = swa_prompt(q, k, vb, rel_bias, attn_sinks[l])
        hp = mix_outputs(hp, u, s_gate, o_b, norm_a_out_g[l], norm_b_out_g[l], w_out[l])
        swa_k_p.append(k[:, -WINDOW:])
        swa_v_p.append(vb[:, -WINDOW:])
        mk, mv = memory_kv(mem_prompt, norm_memsrc_g[l], w_mk[l], w_mv[l])
        mem_k_p.append(mk)
        mem_v_p.append(mv)
        hp = memory_attn(hp, norm_mem_g[l], w_mq[l], w_mo[l], mk, mv)
        hp = peer_ffn(hp, norm_ffn_g[l], peer_wq[l], peer_keys[l], peer_u[l], peer_v[l])

        u, v, q, k, vb = mix_inputs(hs, norm_mix_g[l], w_in[l], ln_v_g[l], ln_v_b[l])
        s_gate = spatial_gate_sample(v, spatial_w[l], spatial_b[l])
        o_b, kbuf, vbuf = swa_sample(q, k, vb, cache_swa_k[l], cache_swa_v[l], rel_bias, attn_sinks[l])
        hs = mix_outputs(hs, u, s_gate, o_b, norm_a_out_g[l], norm_b_out_g[l], w_out[l])
        swa_k_s.append(kbuf)
        swa_v_s.append(vbuf)
        chunk_v_s.append(v)
        hs = memory_attn(hs, norm_mem_g[l], w_mq[l], w_mo[l], cache_mem_k[l], cache_mem_v[l])
        hs = peer_ffn(hs, norm_ffn_g[l], peer_wq[l], peer_keys[l], peer_u[l], peer_v[l])

    y_prompt = rms_norm(hp, norm_final_g)
    y_sample = rms_norm(hs, norm_final_g)
    return (y_prompt, y_sample, jnp.stack(swa_k_p), jnp.stack(swa_v_p), jnp.stack(mem_k_p), jnp.stack(mem_v_p),
            jnp.stack(swa_k_s), jnp.stack(swa_v_s), jnp.stack(chunk_v_s))


_drawn_inputs = setup_inputs


def setup_inputs(seed=0):
    import zlib

    import numpy as np

    out = dict(_drawn_inputs(seed))
    spreads = {}
    factors = {'norm_mix_g': 3.422,
     'ln_v_g': 16.742,
     'ln_v_b': 14.809,
     'spatial_b': 5.39,
     'attn_sinks': 8.0,
     'norm_a_out_g': 4.485,
     'norm_b_out_g': 5.056,
     'norm_mem_g': 8.0,
     'norm_memsrc_g': 5.642,
     'norm_ffn_g': 23.897,
     'norm_final_g': 34.319}
    for name, (base, spread) in spreads.items():
        noise = np.random.default_rng([zlib.crc32(name.encode()), seed]).standard_normal(out[name].shape)
        drawn = base * np.exp(spread * noise) if base else spread * noise
        out[name] = __import__('jax').numpy.asarray(drawn.astype(out[name].dtype))
    for name, factor in factors.items():
        out[name] = (out[name] * factor).astype(out[name].dtype)
    return out
```

```python
import numpy as np
import concourse.bass as bass
from concourse import mybir
from concourse.alu_op_type import AluOpType as ALU

F32 = mybir.dt.float32
F32R = mybir.dt.float32r
U32 = mybir.dt.uint32
ACT = mybir.ActivationFunctionType
AX = mybir.AxisListType

D = 1024
DC = D // 128
SEQ, DEC_B, DEC_L = 1024, 8, 8
SAMPLE = DEC_B * DEC_L
T = SEQ + SAMPLE
NT = SEQ // 128
GRP = 4
NH, NKV, HD = 8, 2, 64
MIXC = 512
KV = NKV * HD
IN_COLS = 2 * MIXC + NH * HD + 2 * KV
Q0, K0 = 2 * MIXC, 2 * MIXC + NH * HD
WIN = 128
SKEYS = WIN + DEC_L
NMEM, MH, MD = 256, 4, 128
MW = MH * MD
PH, PK, TOPK = 8, 128, 16
HK = PH * TOPK
NEG = -1e30
GONE = -3.0e38
EPS = 1e-6
BUCKETS = 32
TOEP = 384
TG = [(0, 364), (364, 364), (728, 360)]
NPAIR = PK // 2
NGRP = DC * len(TG)
H_BANKS = [[0, 1, 2], [3, 4, 5]]
V_BANKS = [6, 7, 0, 1, 2]
C_ID, C_FLIP, C_TRIL, C_BD, C_IOTA, C_OH, C_MASK, C_ROW = 0, 128, 256, 384, 448, 576, 960, 1344
C_W = C_ROW + SAMPLE


def width(t):
    return SAMPLE if isinstance(t, int) and t == NT else 128


def hymba_step_kernel(nc, x, mem, kTc, vc, mkTc, mvc, swa_k_old, swa_v_old, gains, rows, final, w_in, w_out,
                      wsT, wsS, sbias, sbiasS, rel, sinks, w_mq, w_mk, w_mv, w_mo, wq, keysT, u_t, v_w,
                      consts, y, swa_kp, swa_vp, mem_k, mem_v, swa_ks, swa_vs, chunk_v):
    toep_d = nc.dram_tensor("toeplitz_rows", [NH, TOEP], F32).ap()
    x3_d = nc.dram_tensor("x_before_peer", [T, D], F32).ap()
    x3T_d = nc.dram_tensor("x_before_peer_transposed", [128, DC, T], F32).ap()
    xnT_d = nc.dram_tensor("peer_input_transposed", [128, DC, T], F32).ap()
    gates_d = nc.dram_tensor("gates", [PK, PK, T], F32).ap()

    base0 = nc.sbuf_base
    end = nc.sbuf_usable_end
    cursor = [base0]

    def sb(name, shape, dt=F32):
        size = int(np.prod(shape[1:])) * 4
        at = (cursor[0] + 31) // 32 * 32
        cursor[0] = at + size
        assert cursor[0] <= end, (name, cursor[0] - end)
        return nc.alloc_sbuf_tensor_at(name, shape, dt, offset=at)

    cst = sb("cst", [128, C_W])
    gain = sb("gain", [128, 6, DC])
    half = sb("half", [128, 8])
    ssq = sb("ssq", [128, 16])
    rst = sb("rst", [128, 16])
    var = sb("var", [128, 16])
    zero8 = sb("zero8", [128, 8])
    ident = cst[:, C_ID:C_ID + 128]
    common = cursor[0]
    xres = sb("xres", [128, NT + 1, D])
    xn = sb("xn", [128, D])
    xT = sb("xT", [128, DC, 128])
    sq = sb("sq", [128, D])
    sink = sb("sink", [128, NH])
    ab = cursor[0]
    win = sb("win", [128, DC, IN_COLS])
    wout = sb("wout", [128, DC, D])
    bias = sb("bias", [128, NH, 2 * WIN])
    kv = sb("kv", [128, NT + 1, 2 * KV])
    kTa = sb("kTa", [128, 2 * WIN])
    ktile = sb("ktile", [128, KV])
    z = sb("z", [128, 2 * MIXC])
    qT = sb("qT", [128, 4, 128])
    sc = sb("sc", [128, NH, 2 * WIN])
    PT = sb("PT", [128, NH, 2, 128])
    yA = sb("yA", [128, 2 * MIXC])
    yT = sb("yT", [128, DC, 128])
    vln = sb("vln", [128, MIXC])
    lnrow = sb("lnrow", [128, 2, MIXC])
    wsTs = sb("wsTs", [128, GRP, 128])
    wsSs = sb("wsSs", [SAMPLE, GRP, SAMPLE])
    sbs = sb("sbs", [128, GRP])
    sbsS = sb("sbsS", [SAMPLE, GRP])
    bnst = sb("bnst", [128, GRP, 6])
    bnag = sb("bnag", [128, GRP, 2])
    lnr = sb("lnr", [128, GRP])
    mx = sb("mx", [128, 4, NH])
    den = sb("den", [128, 2, NH])
    relS = sb("relS", [BUCKETS, NH])
    toepS = PT[0:NH, :, :, :].rearrange("p a b c -> p (a b c)")[:, 0:TOEP]
    hank = sc
    kTc_s = sb("kTc_s", [128, DEC_B, WIN])
    cursor[0] = ab
    vc_s = sb("vc_s", [128, DEC_B, KV])
    vnew = sb("vnew", [DEC_L, DEC_B, KV])
    biasS = sb("biasS", [SAMPLE, NH, SKEYS])
    STm = sb("STm", [128, 512])
    STn = sb("STn", [DEC_L, 512])
    PTm = sb("PTm", [128, 512])
    PTn = sb("PTn", [DEC_L, 512])
    oTs = sb("oTs", [HD, 512])
    next_w = cursor[0]
    assert next_w + 2 * DC * MW * 4 <= ab + DC * IN_COLS * 4
    cursor[0] = ab
    mkT = sb("mkT", [128, MH, NMEM])
    mkv = sb("mkv", [128, 2, 2, MW])
    qTm = sb("qTm", [128, MH, 128])
    PTb = sb("PTb", [128, MH, 2, 128])
    Pm = sb("Pm", [128, MH, NMEM])
    mxb = sb("mxb", [128, 4, MH])
    assert cursor[0] <= next_w
    cursor[0] = next_w
    wmk = sb("wmk", [128, DC, MW])
    wmv = sb("wmv", [128, DC, MW])
    wmq = sb("wmq", [128, DC, MW])
    wmo = sb("wmo", [128, MH, D])
    mkTc_s = sb("mkTc_s", [128, DEC_B, MH, NMEM])
    mvc_s = sb("mvc_s", [128, DEC_B, 2, MW])
    oTb = sb("oTb", [128, MH, 128])
    memx = Pm[:, :, :].rearrange("p a b -> p (a b)")
    cursor[0] = common
    gs = sb("gs", [128, PK, 128])
    after_gs = cursor[0]
    xc = sb("xc", [128, D])
    qtok = sb("qtok", [128, 512])
    assert cursor[0] <= next_w
    cursor[0] = next_w
    wqs = sb("wqs", [128, DC, 2 * PH * 128])
    kys = sb("kys", [128, 2 * PH, PK])
    xnc = sb("xnc", [128, D])
    xTc = sb("xTc", [128, DC, 128])
    x3T = sb("x3T", [128, DC, 128])
    qpT = sb("qpT", [128, 2 * PH, 128])
    skey = sb("skey", [128, 2 * PH, PK])
    cand = sb("cand", [128, PH, TOPK * TOPK])
    oneA = sb("oneA", [128, 4, 4, 128])
    oneB = sb("oneB", [128, 4, 4, 128])
    v16 = sb("v16", [128, 2 * PH, TOPK])
    i16 = sb("i16", [128, 2 * PH, TOPK], U32)
    top = sb("top", [128, PH, TOPK])
    pos = sb("pos", [128, PH, TOPK], U32)
    prow = sb("prow", [128, 2, HK], U32)
    sel = sb("sel", [128, 3, HK])
    selT = sb("selT", [128, 3, 128])
    i16f = sb("i16f", [128, PH, TOPK])
    gsum = sb("gsum", [128, 2, PH])
    pick = [one[:, :, :, :].rearrange("p a b c -> p (a b c)") for one in (oneB, oneA)]
    cursor[0] = common
    acc = sb("acc", [128, DC, T])
    vh = sb("vh", [128, 2, D], F32R)
    vl = sb("vl", [128, 2, D], F32R)
    hid = sb("hid", [128, 2, T])
    gp = sb("gp", [128, 2, T])
    at_w = cursor[0]
    assert at_w >= after_gs
    wh = [sb(f"wh{i}", [128, 2, T], F32R) for i in range(2)]
    wl = [sb(f"wl{i}", [128, 2, T], F32R) for i in range(2)]
    ur = sb("ur", [128, 2, D])
    vr = sb("vr", [128, 2, D])
    assert cursor[0] <= next_w + DC * 2 * PH * 128 * 4
    xh = sb("xh", [128, DC, T], F32R)
    xl = sb("xl", [128, DC, T], F32R)
    uh = sb("uh", [128, 2, D], F32R)
    ul = sb("ul", [128, 2, D], F32R)
    cursor[0] = at_w
    xf = sb("xf", [128, DC, T])
    cursor[0] = at_w
    fgain = sb("fgain", [128, D])
    yo = sb("yo", [128, 2, D])
    ysq = sb("ysq", [128, D])

    ps = nc.alloc_psum_tensor("ps", [128, 8, 512], F32)

    def banks(a, n):
        return ps[:, a:a + n, :].rearrange("p a b -> p (a b)")

    sems = {}

    def sem(name):
        if name not in sems:
            sems[name] = nc.alloc_semaphore(name)
        return sems[name]

    def need(e, name, value):
        if not (isinstance(value, int) and value <= 0):
            e.wait_ge(sem(name), value)

    class Chain:

        def __init__(self, e, name):
            self.e, self.name, self.base, self.k, self.off = e, name, 0, 0, 0

        def __call__(self, ins):
            self.mark(ins)
            self.wait()

        def mark(self, ins):
            ins.then_inc(sem(self.name), 1)
            self.k += 1

        def wait(self):
            self.e.wait_ge(sem(self.name), self.off + (self.base + self.k))

        def enter(self, i, start, per):
            self.base += self.k - start * per
            self.k = 0
            self.off, self.per = i * per, per

        def leave(self, end):
            assert self.k == self.per, (self.name, self.k, self.per)
            self.base += end * self.per
            self.k, self.off = 0, 0

    class Drained:

        def __init__(self, e):
            self.e = e

        def __call__(self, ins):
            self.e.drain()

        def mark(self, ins):
            pass

        def wait(self):
            self.e.drain()

    SEEN = []

    def seen(e, name):
        e.sem_inc(sem(name), 1)
        if name not in SEEN:
            SEEN.append(name)

    def wide(ap, n):
        return ap.unsqueeze(len(ap.shape)).to_broadcast([*ap.shape, n])

    CONSTS_IN = 16 * 7
    def known(t, v):
        return isinstance(t, int) and t == v

    LAST = NT


    def pe_transposes(src, dst, p, done):
        for dc in range(DC):
            i = nc.tensor.transpose(dst[:, dc * 128:dc * 128 + p], src[0:p, dc * 128:(dc + 1) * 128],
                                    ident[0:p, 0:p])
        i.then_inc(sem(done), 1)

    def mm_sum(out, pairs, done=None):
        for k, (lhsT, rhs) in enumerate(pairs):
            i = nc.tensor.matmul(out, lhsT, rhs, start=(k == 0), stop=(k == len(pairs) - 1))
        if done:
            i.then_inc(sem(done), 1)

    def a_pe(e, t, n):
        p = width(t)
        if t is not None and not (isinstance(t, int) and t == 0):
            need(e, "a_y_ready", t)
            pe_transposes(yA, banks(0, 2), width(t - 1) if isinstance(t, int) else 128, "a_yt")
        if t is not None:
            e.wait_ge(sem("a_kT"), t + 1)
            e.wait_ge(sem("a_q"), t + 1)
            need(e, "a_o_ready", t)
            if isinstance(t, int) and t == LAST:
                e.wait_ge(sem("s_in"), 16 * 2)
                for kvh in range(NKV):
                    r = slice(kvh * HD, (kvh + 1) * HD)
                    for b in range(DEC_B):
                        c = slice(b * DEC_L, (b + 1) * DEC_L)
                        q = qT[r, :, c]
                        o = ps[:, 4 + 2 * kvh, 0:256].rearrange("p (c t) -> p c t", t=SAMPLE)
                        nc.tensor.matmul(o[:, :, c], kTc_s[r, b, :], q, start=True, stop=True)
                        o = ps[0:DEC_L, 5 + 2 * kvh, 0:256].rearrange("p (c t) -> p c t", t=SAMPLE)
                        i = nc.tensor.matmul(o[:, :, c], kTa[r, WIN + b * DEC_L:WIN + (b + 1) * DEC_L], q,
                                             start=True, stop=True)
                i.then_inc(sem("s_st"), 1)
                e.wait_ge(sem("s_st_sb"), 4)
                for h in range(NH):
                    o = ps[0:SAMPLE, 4 + h // 2, (h % 2) * 256:(h % 2) * 256 + SKEYS]
                    nc.tensor.transpose(o[:, 0:WIN], STm[:, h * SAMPLE:(h + 1) * SAMPLE], ident)
                    i = nc.tensor.transpose(o[:, WIN:SKEYS], STn[:, h * SAMPLE:(h + 1) * SAMPLE],
                                            ident[0:DEC_L, 0:DEC_L])
                    if h % 2:
                        i.then_inc(sem("a_s"), 1)
            else:
                first = isinstance(t, int) and t == 0
                for h in range(NH):
                    r = slice((h // 4) * HD, (h // 4 + 1) * HD)
                    o = ps[:, 4 + h // 2, (h % 2) * 256:(h % 2) * 256 + 256]
                    if first:
                        i = nc.tensor.matmul(o[:, WIN:2 * WIN], qT[r, h % 4, :], kTa[r, WIN:2 * WIN], start=True, stop=True)
                    else:
                        i = nc.tensor.matmul(o, qT[r, h % 4, :], kTa[r, :],
                                             start=True, stop=True)
                    if h % 2:
                        i.then_inc(sem("a_s"), 1)
        if t is not None and not (isinstance(t, int) and t == 0):
            e.wait_ge(sem("a_yT"), t * 2)
            e.wait_ge(sem("w_out_in"), 16)
            e.wait_ge(sem("a_q"), t + 1)
            pp = width(t - 1) if isinstance(t, int) else 128
            for half_ in range(2):
                c = slice(half_ * 512, half_ * 512 + 512)
                mm_sum(ps[0:pp, 2 + half_, :], [(yT[:, dc, 0:pp], wout[:, dc, c]) for dc in range(DC)], "a_out")
        if t is not None:
            e.wait_ge(sem("a_vln"), t + 1)
            if isinstance(t, int) and t == 0:
                e.wait_ge(sem("ws_ready"), 2)
            w = wsSs if (isinstance(t, int) and t == LAST) else wsTs
            for g in range(GRP):
                i = nc.tensor.matmul(ps[0:p, 0, g * 128:(g + 1) * 128], w[0:p, g, 0:p],
                                     vln[0:p, g * 128:(g + 1) * 128], start=True, stop=True)
            i.then_inc(sem("a_gate"), 1)
            e.wait_ge(sem("a_exp"), (t + 1) * (NH + 1))
            if isinstance(t, int) and t == LAST:
                for h in range(NH):
                    nc.tensor.transpose(ps[:, 4, h * SAMPLE:(h + 1) * SAMPLE], sc[0:SAMPLE, h, 0:WIN], ident[0:SAMPLE, 0:SAMPLE])
                    i = nc.tensor.transpose(ps[0:DEC_L, 5, h * SAMPLE:(h + 1) * SAMPLE], sc[0:SAMPLE, h, WIN:SKEYS],
                                            ident[0:SAMPLE, 0:SAMPLE])
                i.then_inc(sem("a_pt"), 4)
            else:
                for h in range(NH):
                    for kb in range(2):
                        if kb or not first:
                            o = ps[:, 4 + h // 2, (h % 2) * 256 + kb * 128:(h % 2) * 256 + kb * 128 + 128]
                            i = nc.tensor.transpose(o, sc[:, h, kb * 128:(kb + 1) * 128], ident)
                    if h % 2:
                        i.then_inc(sem("a_pt"), 1)
        if n is not None:
            np_ = width(n)
            e.wait_ge(sem("a_xn"), n + 1)
            need(e, "a_yA", n)
            if known(n, 0):
                e.wait_ge(sem("const_in"), CONSTS_IN)
            pe_transposes(xn, banks(0, 2), np_, "a_tx")
            e.wait_ge(sem("a_xT"), (n + 1) * 2)
            if isinstance(n, int) and n == 0:
                e.wait_ge(sem("w_in_in"), 16)
            need(e, "a_xmid", (n - 1) * 2)
            for half_ in range(2):
                c = slice(half_ * 512, half_ * 512 + 512)
                mm_sum(ps[0:np_, 2 + half_, :], [(xT[:, dc, 0:np_], win[:, dc, c]) for dc in range(DC)], "a_z")
        if t is not None:
            e.wait_ge(sem("a_ptA"), t + 1)
            e.wait_ge(sem("a_ptV"), t + 1)
            if isinstance(t, int) and t == LAST:
                e.wait_ge(sem("s_vnew"), 16)
                for kvh in range(NKV):
                    vcols = slice(kvh * HD, (kvh + 1) * HD)
                    for b in range(DEC_B):
                        c = slice(b * DEC_L, (b + 1) * DEC_L)
                        view = lambda ap: ap.rearrange("p (h t) -> p h t", t=SAMPLE)[:, kvh * 4:kvh * 4 + 4, c]
                        o = view(ps[0:HD, 6, :])
                        nc.tensor.matmul(o, vc_s[:, b, vcols], view(PTm[:, :]), start=True, stop=False)
                        i = nc.tensor.matmul(o, vnew[:, b, vcols], view(PTn[:, :]), start=False, stop=True)
                i.then_inc(sem("s_ot"), 1)
                e.wait_ge(sem("s_ot_sb"), 1)
                for h in range(NH):
                    i = nc.tensor.transpose(ps[0:SAMPLE, 4, h * HD:(h + 1) * HD], oTs[:, h * SAMPLE:(h + 1) * SAMPLE],
                                            ident[0:HD, 0:HD])
                i.then_inc(sem("a_pv"), 1)
            else:
                for h in range(NH):
                    vcols = slice(KV + (h // 4) * HD, KV + (h // 4 + 1) * HD)
                    o = ps[:, 4, h * HD:(h + 1) * HD]
                    if not first:
                        nc.tensor.matmul(o, PT[:, h, 0, :], kv[:, bass.ds(t - 1, 1), vcols].squeeze(1) if not isinstance(t, int) else kv[:, t - 1, vcols],
                                         start=True, stop=False)
                    i = nc.tensor.matmul(o, PT[:, h, 1, :], kv[:, bass.ds(t, 1), vcols].squeeze(1) if not isinstance(t, int) else kv[:, t, vcols],
                                         start=first, stop=True)
                i.then_inc(sem("a_pv"), 1)
        if n is not None:
            e.wait_ge(sem("a_gelu"), (n + 1) * 2)
            mm_sum(ps[0:np_, 2, 0:2 * KV], [(xT[:, dc, 0:np_], win[:, dc, K0:K0 + 2 * KV]) for dc in range(DC)], "a_kv")
            for c in range(4):
                mm_sum(ps[:, 3, c * 128:c * 128 + np_],
                       [(win[:, dc, Q0 + c * 128:Q0 + (c + 1) * 128], xT[:, dc, 0:np_]) for dc in range(DC)],
                       "a_qmm" if c == 3 else None)
            e.wait_ge(sem("a_kvsb"), (n + 1) * 2)
            if t is not None:
                e.wait_ge(sem("a_ptA"), t + 1)
                e.wait_ge(sem("a_ptV"), t + 1)
            nc.tensor.transpose(ps[:, 5, 0:np_], ktile[0:np_, :], ident[0:np_, 0:np_]).then_inc(sem("a_ktr"), 1)

    def at(ap, t):
        return ap[:, t, :] if isinstance(t, int) else ap[:, bass.ds(t, 1), :].squeeze(1)

    def x_square(e, m, src, p, col, name):
        e.drain()
        need(e, "a_rstd", m)
        nc.scalar.activation(sq[0:p, :], src, ACT.Square, accum_out=ssq[0:p, col:col + 1]).then_inc(sem(name), 1)

    def a_act(e, t, n):
        p = width(t)
        if t is not None:
            sample = isinstance(t, int) and t == LAST
            first = isinstance(t, int) and t == 0
            lo, hi = (WIN, 2 * WIN) if first else (0, SKEYS if sample else 2 * WIN)
            if sample:
                e.wait_ge(sem("s_st"), 1)
                for kvh in range(NKV):
                    c = slice(kvh * 256, (kvh + 1) * 256)
                    nc.scalar.activation(STm[:, c], ps[:, 4 + 2 * kvh, 0:256], ACT.Copy).then_inc(sem("s_st_sb"), 1)
                    nc.scalar.activation(STn[:, c], ps[0:DEC_L, 5 + 2 * kvh, 0:256], ACT.Copy).then_inc(sem("s_st_sb"), 1)
            e.wait_ge(sem("a_stat"), t + 1)
            for h in range(NH):
                nc.scalar.activation(sc[0:p, h, lo:hi], sc[0:p, h, lo:hi], ACT.Exp, bias=mx[0:p, 1, h:h + 1],
                                     accum_out=mx[0:p, 3, h:h + 1]).then_inc(sem("a_exp"), 1)
            need(e, "a_den", t)
            nc.scalar.activation(den[0:p, 0, :], mx[0:p, 2, :], ACT.Exp).then_inc(sem("a_exp"), 1)
            e.wait_ge(sem("a_pt"), (t + 1) * 4)
            if sample:
                nc.scalar.activation(PTm[:], ps[:, 4, :], ACT.Copy).then_inc(sem("a_ptA"), 1)
            elif first:
                nc.scalar.activation(PT[:, 4:8, 1, :], ps[:, 6:8, :].rearrange("p a (h k q) -> p (a h) k q", h=2, k=2)[:, :, 1, :], ACT.Copy).then_inc(sem("a_ptA"), 1)
            else:
                nc.scalar.activation(PT[:, 4:8, :, :].rearrange("p a b c -> p (a b c)"), banks(6, 2), ACT.Copy).then_inc(sem("a_ptA"), 1)
            if sample:
                e.wait_ge(sem("s_ot"), 1)
                nc.scalar.activation(oTs[:], ps[0:HD, 6, :], ACT.Copy).then_inc(sem("s_ot_sb"), 1)
        if n is not None:
            np_ = width(n)
            for half_ in range(2):
                e.wait_ge(sem("a_z"), n * 2 + half_ + 1)
                need(e, "a_yA", n)
                nc.scalar.activation(z[0:np_, half_ * 512:half_ * 512 + 512], ps[0:np_, 2 + half_, :],
                                     ACT.Gelu_apprx_tanh).then_inc(sem("a_gelu"), 1)
            e.wait_ge(sem("a_kv"), n + 1)
            need(e, "a_ktr", n)
            nc.scalar.activation(at(kv, n)[0:np_, :], ps[0:np_, 2, 0:2 * KV], ACT.Copy).then_inc(sem("a_kvsb"), 1)
            nc.scalar.activation(ktile[0:np_, :], ps[0:np_, 2, 0:KV], ACT.Copy).then_inc(sem("a_kvsb"), 1)
            e.wait_ge(sem("a_qmm"), n + 1)
            nc.scalar.activation(qT[:, :, 0:np_], ps[:, 3, :].rearrange("p (c t) -> p c t", c=4)[:, :, 0:np_], ACT.Copy,
                                 scale=float(HD) ** -0.5).then_inc(sem("a_q"), 1)
            e.wait_ge(sem("a_ktr"), n + 1)
            if not known(n, 0):
                e.wait_ge(sem("a_kT"), n)
                nc.scalar.activation(kTa[:, 0:WIN], kTa[:, WIN:2 * WIN], ACT.Copy)
                e.drain()
            nc.scalar.activation(kTa[:, WIN:WIN + np_], ps[:, 5, 0:np_], ACT.Copy).then_inc(sem("a_kT"), 1)
        if t is not None:
            e.wait_ge(sem("a_yA"), t + 1)
            nc.scalar.activation(sq[0:p, 0:512], yA[0:p, 0:512], ACT.Square, accum_out=ssq[0:p, 1:2]).then_inc(sem("a_yssq"), 1)
            e.wait_ge(sem("a_o_ready"), t + 1)
            nc.scalar.activation(sq[0:p, 512:1024], yA[0:p, 512:1024], ACT.Square, accum_out=ssq[0:p, 2:3]).then_inc(sem("a_yssq"), 1)
        m = 0 if n is None and t is None else (None if n is None else n + 1)
        if m is not None and not (isinstance(m, int) and m > LAST):
            if isinstance(m, int) and m == 0:
                e.wait_ge(sem("x_in_0"), 16)
            if isinstance(m, int) and m == 1:
                e.wait_ge(sem("tokens_ws_in"), 16 * 4)
            x_square(e, m, at(xres, m)[0:width(m), :], width(m), 0, "a_xssq")

    def rsqrt_mean(ch, src, dst, mean, p, c0, c1):
        ch(nc.gpsimd.tensor_scalar(var[0:p, c0:c1], src, mean, EPS, ALU.mult, ALU.add))
        return nc.gpsimd.tensor_tensor(dst, var[0:p, c0:c1], half[0:p, 0:c1 - c0], ALU.pow)

    def a_pool(e, ch, t, n):
        p = width(t)
        if n is not None:
            np_ = width(n)
            e.wait_ge(sem("a_lnvar"), n + 1)
            seen(e, "a_lnvar_seen")
            ch(nc.gpsimd.tensor_scalar(var[0:np_, 4:8], bnag[0:np_, :, 1], 1.0, EPS, ALU.mult, ALU.add))
            nc.gpsimd.tensor_tensor(lnr[0:np_, :], var[0:np_, 4:8], half[0:np_, 0:GRP], ALU.pow).then_inc(sem("a_lnr"), 1)
        if t is not None:
            e.wait_ge(sem("a_yssq"), (t + 1) * 2)
            seen(e, "a_yssq_seen")
            rsqrt_mean(ch, ssq[0:p, 1:3], rst[0:p, 1:3], 1.0 / MIXC, p, 1, 3).then_inc(sem("a_yrstd"), 1)
        m = 0 if n is None and t is None else (None if n is None else n + 1)
        if m is not None and not (isinstance(m, int) and m > LAST):
            mp = width(m)
            e.wait_ge(sem("a_xssq"), m + 1)
            need(e, "a_xn", m)
            seen(e, "a_xssq_seen")
            rsqrt_mean(ch, ssq[0:mp, 0:1], rst[0:mp, 0:1], 1.0 / D, mp, 0, 1).then_inc(sem("a_rstd"), 1)

    def gained(dst, src, which, p, lo, cnt):
        return nc.vector.tensor_tensor(dst[:, lo:lo + cnt, 0:p],
                                       src.rearrange("p (c t) -> p c t", t=128)[:, lo:lo + cnt, 0:p],
                                       wide(gain[:, which, lo:lo + cnt], p), ALU.mult)

    def a_dve(e, ch, t, n):
        p = width(t)
        sample = isinstance(t, int) and t == LAST
        first = isinstance(t, int) and t == 0
        if n is not None:
            np_ = width(n)
            e.wait_ge(sem("a_rstd"), n + 1)
            need(e, "a_tx", n)
            nc.vector.tensor_scalar(xn[0:np_, :], at(xres, n)[0:np_, :], rst[0:np_, 0:1], None, ALU.mult).then_inc(sem("a_xn"), 1)
        if t is not None and not first:
            pp = width(t - 1) if isinstance(t, int) else 128
            e.wait_ge(sem("a_yt"), t)
            need(e, "a_out", (t - 1) * 2)
            for k in range(2):
                gained(yT, banks(0, 2), 1, pp, k * 4, 4).then_inc(sem("a_yT"), 1)
        if t is not None:
            lo, hi = (WIN, 2 * WIN) if first else (0, SKEYS if sample else 2 * WIN)
            if first:
                e.wait_ge(sem("bias_ready"), 4)
            if sample:
                e.wait_ge(sem("s_bias"), 8)
            b = biasS if sample else bias
            for k in range(4):
                e.wait_ge(sem("a_s"), t * 4 + k + 1)
                ch.mark(nc.vector.tensor_tensor(sc[0:p, 2 * k:2 * k + 2, lo:hi],
                                                ps[0:p, 4 + k, :].rearrange("p (h s) -> p h s", h=2)[:, :, lo:hi],
                                                b[0:p, 2 * k:2 * k + 2, lo:hi], ALU.add))
            ch.wait()
            ch(nc.vector.tensor_reduce(mx[0:p, 0, :], sc[0:p, :, lo:hi], AX.X, ALU.max))
            ch(nc.vector.tensor_tensor(mx[0:p, 0, :], mx[0:p, 0, :], sink[0:p, :], ALU.max))
            ch.mark(nc.vector.tensor_tensor(mx[0:p, 2, :], sink[0:p, :], mx[0:p, 0, :], ALU.subtract))
            nc.vector.tensor_scalar(mx[0:p, 1, :], mx[0:p, 0, :], -1.0, None, ALU.mult).then_inc(sem("a_stat"), 1)
        if t is not None and not first:
            for k in range(2):
                c = slice(k * 512, k * 512 + 512)
                e.wait_ge(sem("a_out"), (t - 1) * 2 + k + 1)
                nc.vector.tensor_tensor(at(xres, t - 1)[0:pp, c], at(xres, t - 1)[0:pp, c], ps[0:pp, 2 + k, :],
                                        ALU.add).then_inc(sem("a_xmid"), 1)
        if t is not None:
            e.wait_ge(sem("a_gate"), t + 1)
            sbv = sbsS if sample else sbs
            for g in range(GRP):
                c = slice(g * 128, (g + 1) * 128)
                i = nc.vector.scalar_tensor_tensor(yA[0:p, c], ps[0:p, 0, c], sbv[0:p, g:g + 1], z[0:p, c],
                                                   op0=ALU.add, op1=ALU.mult)
                if g < GRP - 1:
                    ch.mark(i)
                else:
                    i.then_inc(sem("a_yA"), 1)
            e.wait_ge(sem("a_pt"), (t + 1) * 4)
            if sample:
                nc.vector.tensor_copy(PTn[:], ps[0:DEC_L, 5, :]).then_inc(sem("a_ptV"), 1)
            elif first:
                nc.vector.tensor_copy(PT[:, 0:4, 1, :], ps[:, 4:6, :].rearrange("p a (h k q) -> p (a h) k q", h=2, k=2)[:, :, 1, :]).then_inc(sem("a_ptV"), 1)
            else:
                nc.vector.tensor_copy(PT[:, 0:4, :, :].rearrange("p a b c -> p (a b c)"), banks(4, 2)).then_inc(sem("a_ptV"), 1)
        if n is not None:
            e.wait_ge(sem("a_tx"), n + 1)
            need(e, "a_qmm", n)
            for k in range(2):
                gained(xT, banks(0, 2), 0, np_, k * 4, 4).then_inc(sem("a_xT"), 1)
        if t is not None:
            e.wait_ge(sem("a_exp"), (t + 1) * (NH + 1))
            ch(nc.vector.tensor_tensor(den[0:p, 1, :], mx[0:p, 3, :], den[0:p, 0, :], ALU.add))
            i = nc.vector.reciprocal(den[0:p, 1, :], den[0:p, 1, :])
            i.then_inc(sem("a_den"), 1)
            e.wait_ge(sem("a_den"), t + 1)
            e.wait_ge(sem("a_pv"), t + 1)
            nc.vector.tensor_tensor(yA[0:p, 512:1024].rearrange("p (h d) -> p h d", h=NH),
                                    ps[0:p, 4, :].rearrange("p (h d) -> p h d", h=NH), wide(den[0:p, 1, :], HD),
                                    ALU.mult).then_inc(sem("a_o_ready"), 1)
        if n is not None:
            e.wait_ge(sem("a_gelu"), (n + 1) * 2)
            need(e, "a_gate", n)
            for g in range(GRP):
                ch.mark(nc.vector.bn_stats(bnst[0:np_, g, :], z[0:np_, 512 + g * 128:512 + (g + 1) * 128]))
            ch.wait()
            for g in range(GRP):
                i = nc.vector.bn_aggr(bnag[0:np_, g, :], bnst[0:np_, g, :])
                if g < GRP - 1:
                    ch.mark(i)
                else:
                    i.then_inc(sem("a_lnvar"), 1)
            e.wait_ge(sem("a_lnvar"), n + 1)
            e.wait_ge(sem("a_lnr"), n + 1)
            for g in range(GRP):
                c = slice(g * 128, (g + 1) * 128)
                ch.mark(nc.vector.tensor_scalar(vln[0:np_, c], z[0:np_, 512 + g * 128:512 + (g + 1) * 128],
                                                bnag[0:np_, g, 0:1], lnr[0:np_, g:g + 1], ALU.subtract, ALU.mult))
            ch.wait()
            ch(nc.vector.tensor_tensor(vln[0:np_, :], vln[0:np_, :], lnrow[0:np_, 0, :], ALU.mult))
            nc.vector.tensor_tensor(vln[0:np_, :], vln[0:np_, :], lnrow[0:np_, 1, :], ALU.add).then_inc(sem("a_vln"), 1)
        if t is not None:
            e.wait_ge(sem("a_yrstd"), t + 1)
            ch.mark(nc.vector.tensor_scalar(yA[0:p, 0:512], yA[0:p, 0:512], rst[0:p, 1:2], None, ALU.mult))
            nc.vector.tensor_scalar(yA[0:p, 512:1024], yA[0:p, 512:1024], rst[0:p, 2:3], None, ALU.mult).then_inc(sem("a_y_ready"), 1)

    def a_pe_tail(e):
        e.wait_ge(sem("a_y_ready"), NT + 1)
        pe_transposes(yA, banks(0, 2), SAMPLE, "a_yt")
        e.wait_ge(sem("a_yT"), (NT + 1) * 2)
        for k in range(2):
            c = slice(k * 512, k * 512 + 512)
            mm_sum(ps[0:SAMPLE, 2 + k, :], [(yT[:, dc, 0:SAMPLE], wout[:, dc, c]) for dc in range(DC)], "a_out")

    def a_dve_tail(e):
        e.wait_ge(sem("a_yt"), NT + 1)
        e.wait_ge(sem("a_out"), NT * 2)
        for k in range(2):
            gained(yT, banks(0, 2), 1, SAMPLE, k * 4, 4).then_inc(sem("a_yT"), 1)
        for k in range(2):
            c = slice(k * 512, k * 512 + 512)
            e.wait_ge(sem("a_out"), NT * 2 + k + 1)
            nc.vector.tensor_tensor(xres[0:SAMPLE, NT, c], xres[0:SAMPLE, NT, c], ps[0:SAMPLE, 2 + k, :],
                                    ALU.add).then_inc(sem("a_xmid"), 1)

    def setup_pe(e):
        e.wait_ge(sem("const_in"), CONSTS_IN)
        nc.tensor.matmul(ps[0:NH, 4, 0:TOEP], relS[:, :], cst[0:BUCKETS, C_OH:C_OH + TOEP], start=True,
                         stop=True).then_inc(sem("toep_mm"), 1)
        e.wait_ge(sem("toep_moved"), 16 * 2)
        for k in range(4):
            nc.tensor.matmul(ps[:, 4 + k, :], cst[:, C_FLIP:C_FLIP + 128],
                             hank[:, 2 * k:2 * k + 2, :].rearrange("p a b -> p (a b)"),
                             start=True, stop=True).then_inc(sem("bias_mm"), 1)
        e.wait_ge(sem("bias_ready"), 4)

    def setup_dve(e):
        e.wait_ge(sem("const_in"), CONSTS_IN)
        nc.vector.memset(half[:, :], -0.5).then_inc(sem("half_ready"), 1)
        e.wait_ge(sem("toep_mm"), 1)
        nc.vector.tensor_tensor(toepS, ps[0:NH, 4, 0:TOEP], cst[0:NH, C_MASK:C_MASK + TOEP], ALU.add).then_inc(sem("toep_sb"), 1)
        for k in range(4):
            e.wait_ge(sem("bias_mm"), k + 1)
            nc.vector.tensor_copy(bias[:, 2 * k:2 * k + 2, :].rearrange("p a b -> p (a b)"), ps[:, 4 + k, :]).then_inc(sem("bias_ready"), 1)

    def ws_dve(e):
        e.wait_ge(sem("tokens_ws_in"), 16 * 4)
        nc.vector.tensor_tensor(wsTs[:], wsTs[:], cst[:, C_TRIL:C_TRIL + 128].unsqueeze(1).to_broadcast([128, GRP, 128]),
                                ALU.mult).then_inc(sem("ws_ready"), 1)
        nc.vector.tensor_tensor(wsSs[:], wsSs[:], cst[0:SAMPLE, C_BD:C_BD + SAMPLE].unsqueeze(1).to_broadcast([SAMPLE, GRP, SAMPLE]),
                                ALU.mult).then_inc(sem("ws_ready"), 1)

    def s_bias_pe(e):
        e.wait_ge(sem("bias_ready"), 4)
        e.wait_ge(sem("a_o_ready"), NT)
        e.wait_ge(sem("a_kT"), NT + 1)
        for k in range(4):
            i = nc.tensor.matmul(ps[0:SAMPLE, 4 + k, 0:2 * SKEYS].rearrange("p (h s) -> p h s", h=2),
                                 cst[0:DEC_L, C_ROW:C_ROW + SAMPLE], bias[0:DEC_L, 2 * k:2 * k + 2, 0:SKEYS],
                                 start=True, stop=True)
        i.then_inc(sem("s_bias_mm"), 1)
        e.wait_ge(sem("s_bias"), 8)

    def s_bias_dve(e):
        e.wait_ge(sem("s_bias_mm"), 1)
        for k in range(4):
            nc.vector.tensor_copy(biasS[:, 2 * k:2 * k + 2, :],
                                  ps[0:SAMPLE, 4 + k, 0:2 * SKEYS].rearrange("p (h s) -> p h s", h=2)).then_inc(sem("s_bias"), 2)


    def m_pe(e, m):
        e.wait_ge(sem("m_xn"), m + 1)
        pe_transposes(xn, banks(0, 2), 128, "m_tx")
        e.wait_ge(sem("m_xT"), (m + 1) * 2)
        e.wait_ge(sem("m_w_in"), 16 * 2)
        for k, w in enumerate((wmk, wmv)):
            mm_sum(ps[:, 2 + k, :], [(xT[:, dc, :], w[:, dc, :]) for dc in range(DC)], "m_mm")
        e.wait_ge(sem("m_kv"), (m + 1) * 2)
        for h in range(MH):
            i = nc.tensor.transpose(ps[:, 4, h * 128:(h + 1) * 128], mkv[:, m, 0, h * 128:(h + 1) * 128], ident)
        i.then_inc(sem("m_ktr"), 1)
        e.wait_ge(sem("m_kT"), m + 1)

    def m_act(e, m):
        e.wait_ge(sem("mem_in"), (m + 1) * 16)
        need(e, "m_rstd", m)
        nc.scalar.activation(sq[:], memx, ACT.Square, accum_out=ssq[:, 0:1]).then_inc(sem("m_ssq"), 1)
        for k in range(2):
            e.wait_ge(sem("m_mm"), m * 2 + k + 1)
            nc.scalar.activation(mkv[:, m, k, :], ps[:, 2 + k, :], ACT.Copy).then_inc(sem("m_kv"), 1)
        e.wait_ge(sem("m_ktr"), m + 1)
        nc.scalar.activation(mkT[:, :, m * 128:(m + 1) * 128], ps[:, 4, :].rearrange("p (h t) -> p h t", h=MH),
                             ACT.Copy).then_inc(sem("m_kT"), 1)

    def m_pool(e, ch, m):
        e.wait_ge(sem("m_ssq"), m + 1)
        need(e, "m_xn", m)
        rsqrt_mean(ch, ssq[:, 0:1], rst[:, 0:1], 1.0 / D, 128, 0, 1).then_inc(sem("m_rstd"), 1)

    def m_dve(e, m):
        e.wait_ge(sem("m_rstd"), m + 1)
        need(e, "m_tx", m)
        nc.vector.tensor_scalar(xn[:], memx, rst[:, 0:1], None, ALU.mult).then_inc(sem("m_xn"), 1)
        e.wait_ge(sem("m_tx"), m + 1)
        need(e, "m_mm", m * 2)
        for k in range(2):
            gained(xT, banks(0, 2), 3, 128, k * 4, 4).then_inc(sem("m_xT"), 1)

    def b_pe(e, t, n):
        p = width(t)
        sample = isinstance(t, int) and t == LAST
        if t is not None:
            e.wait_ge(sem("b_q"), t + 1)
            need(e, "b_xmid", t * 2)
            if sample:
                e.wait_ge(sem("b_cache_in"), 32)
                for h in range(MH):
                    for mh in range(2):
                        for b in range(DEC_B):
                            o = (h * 2 + mh) * SAMPLE + b * DEC_L
                            i = nc.tensor.matmul(ps[:, 6, o:o + DEC_L], mkTc_s[:, b, h, mh * 128:(mh + 1) * 128],
                                                 qTm[:, h, b * DEC_L:(b + 1) * DEC_L], start=True, stop=True)
                i.then_inc(sem("s_bst"), 1)
                e.wait_ge(sem("s_bst_sb"), 1)
                for h in range(MH):
                    for mh in range(2):
                        i = nc.tensor.transpose(ps[0:SAMPLE, 4 + h // 2, (h % 2) * 256 + mh * 128:(h % 2) * 256 + mh * 128 + 128],
                                                PTb[:, h, mh, 0:SAMPLE], ident)
            else:
                for h in range(MH):
                    i = nc.tensor.matmul(ps[0:p, 4 + h // 2, (h % 2) * 256:(h % 2) * 256 + 256], qTm[:, h, 0:p],
                                         mkT[:, h, :], start=True, stop=True)
            i.then_inc(sem("b_s"), 1)
        if n is not None:
            np_ = width(n)
            e.wait_ge(sem("b_xn"), n + 1)
            pe_transposes(xn, banks(0, 2), np_, "b_tx")
            e.wait_ge(sem("b_xT"), (n + 1) * 2)
            if isinstance(n, int) and n == 0:
                e.wait_ge(sem("b_w_in"), 16 * 2)
            for c in range(MH):
                mm_sum(ps[:, 2, c * 128:c * 128 + np_],
                       [(wmq[:, dc, c * 128:(c + 1) * 128], xT[:, dc, 0:np_]) for dc in range(DC)],
                       "b_qmm" if c == MH - 1 else None)
        if t is not None:
            e.wait_ge(sem("b_p"), t + 1)
            for h in range(MH):
                for mh in range(2):
                    i = nc.tensor.transpose(ps[:, 6 + h // 2, (h % 2) * 256 + mh * 128:(h % 2) * 256 + mh * 128 + p],
                                            Pm[0:p, h, mh * 128:(mh + 1) * 128], ident[0:p, 0:p])
            i.then_inc(sem("b_pt"), 1)
            e.wait_ge(sem("b_ptA"), t + 1)
            e.wait_ge(sem("b_ptV"), t + 1)
            for h in range(MH):
                if sample:
                    for b in range(DEC_B):
                        c = slice(b * DEC_L, (b + 1) * DEC_L)
                        for mh in range(2):
                            i = nc.tensor.matmul(ps[:, 3, h * 128 + b * DEC_L:h * 128 + (b + 1) * DEC_L],
                                                 mvc_s[:, b, mh, h * 128:(h + 1) * 128], PTb[:, h, mh, c],
                                                 start=(mh == 0), stop=(mh == 1))
                else:
                    for mh in range(2):
                        i = nc.tensor.matmul(ps[:, 3, h * 128:h * 128 + p], mkv[:, mh, 1, h * 128:(h + 1) * 128],
                                             PTb[:, h, mh, 0:p], start=(mh == 0), stop=(mh == 1))
            i.then_inc(sem("b_pv"), 1)
            e.wait_ge(sem("b_oT"), t + 1)
            for k in range(2):
                mm_sum(ps[0:p, 4 + k, :], [(oTb[:, h, 0:p], wmo[:, h, k * 512:(k + 1) * 512]) for h in range(MH)], "b_out")

    def b_act(e, t, n):
        p = width(t)
        sample = isinstance(t, int) and t == LAST
        if t is not None:
            if sample:
                e.wait_ge(sem("s_bst"), 1)
                nc.scalar.activation(PTb[:, :, :, 0:SAMPLE], ps[:, 6, :].rearrange("p (h m t) -> p h m t", h=MH, m=2),
                                     ACT.Copy).then_inc(sem("s_bst_sb"), 1)
            e.wait_ge(sem("b_stat"), t + 1)
            need(e, "b_pt", t)
            for h in range(MH):
                nc.scalar.activation(Pm[0:p, h, :], ps[0:p, 4 + h // 2, (h % 2) * 256:(h % 2) * 256 + 256], ACT.Exp,
                                     bias=mxb[0:p, 1, h:h + 1], accum_out=mxb[0:p, 2, h:h + 1]).then_inc(sem("b_exp"), 1)
        if n is not None:
            np_ = width(n)
            e.wait_ge(sem("b_qmm"), n + 1)
            need(e, "b_s", n)
            nc.scalar.activation(qTm[:, :, 0:np_], ps[:, 2, :].rearrange("p (c t) -> p c t", c=MH)[:, :, 0:np_], ACT.Copy,
                                 scale=float(MD) ** -0.5).then_inc(sem("b_q"), 1)
        if t is not None:
            e.wait_ge(sem("b_pt"), t + 1)
            nc.scalar.activation(PTb[:, 2:4, :, 0:p].rearrange("p a b c -> p (a b) c"),
                                 ps[:, 7, :].rearrange("p (a c) -> p a c", c=128)[:, :, 0:p], ACT.Copy).then_inc(sem("b_ptA"), 1)
        m = 0 if n is None and t is None else (None if n is None else n + 1)
        if m is not None and not (isinstance(m, int) and m > LAST):
            need(e, "b_rstd", m)
            mp = width(m)
            nc.scalar.activation(sq[0:mp, :], at(xres, m)[0:mp, :], ACT.Square, accum_out=ssq[0:mp, 0:1]).then_inc(sem("b_xssq"), 1)

    def b_pool(e, ch, t, n):
        m = 0 if n is None and t is None else (None if n is None else n + 1)
        if m is not None and not (isinstance(m, int) and m > LAST):
            mp = width(m)
            e.wait_ge(sem("b_xssq"), m + 1)
            need(e, "b_xn", m)
            seen(e, "b_xssq_seen")
            rsqrt_mean(ch, ssq[0:mp, 0:1], rst[0:mp, 0:1], 1.0 / D, mp, 0, 1).then_inc(sem("b_rstd"), 1)

    def b_dve(e, ch, t, n):
        p = width(t)
        if n is not None:
            np_ = width(n)
            e.wait_ge(sem("b_rstd"), n + 1)
            need(e, "b_tx", n)
            nc.vector.tensor_scalar(xn[0:np_, :], at(xres, n)[0:np_, :], rst[0:np_, 0:1], None, ALU.mult).then_inc(sem("b_xn"), 1)
        if t is not None:
            e.wait_ge(sem("b_s"), t + 1)
            ch(nc.vector.tensor_reduce(mxb[0:p, 0, :], banks(4, 2)[0:p, :].rearrange("p (h s) -> p h s", h=MH), AX.X, ALU.max))
            nc.vector.tensor_scalar(mxb[0:p, 1, :], mxb[0:p, 0, :], -1.0, None, ALU.mult).then_inc(sem("b_stat"), 1)
        if n is not None:
            e.wait_ge(sem("b_tx"), n + 1)
            need(e, "b_qmm", n)
            for k in range(2):
                gained(xT, banks(0, 2), 2, np_, k * 4, 4).then_inc(sem("b_xT"), 1)
        if t is not None:
            e.wait_ge(sem("b_exp"), (t + 1) * MH)
            ch(nc.vector.reciprocal(mxb[0:p, 3, :], mxb[0:p, 2, :]))
            nc.vector.tensor_tensor(Pm[0:p, :, :], Pm[0:p, :, :], wide(mxb[0:p, 3, :], NMEM), ALU.mult).then_inc(sem("b_p"), 1)
            e.wait_ge(sem("b_pt"), t + 1)
            nc.vector.tensor_copy(PTb[:, 0:2, :, 0:p].rearrange("p a b c -> p (a b) c"),
                                  ps[:, 6, :].rearrange("p (a c) -> p a c", c=128)[:, :, 0:p]).then_inc(sem("b_ptV"), 1)
            e.wait_ge(sem("b_pv"), t + 1)
            nc.vector.tensor_copy(oTb[:, :, 0:p], ps[:, 3, :].rearrange("p (h t) -> p h t", h=MH)[:, :, 0:p]).then_inc(sem("b_oT"), 1)
            for k in range(2):
                c = slice(k * 512, k * 512 + 512)
                e.wait_ge(sem("b_out"), t * 2 + k + 1)
                nc.vector.tensor_tensor(at(xres, t)[0:p, c], at(xres, t)[0:p, c], ps[0:p, 4 + k, :], ALU.add).then_inc(sem("b_xmid"), 1)


    def q_transposes(e, n, k):
        np_ = width(n)
        e.wait_ge(sem("c_qtok"), n * 4 + k + 1)
        for c in range(4):
            i = nc.tensor.transpose(ps[:, 2 + k, c * 128:c * 128 + np_], qtok[0:np_, c * 128:(c + 1) * 128],
                                    ident[0:np_, 0:np_])
        i.then_inc(sem("c_qt"), 1)

    G_BANK = [6, 7, 2, 3]

    def c_pe(e, t, n):
        if n is not None:
            np_ = width(n)
            e.wait_ge(sem("c_xn"), n + 1)
            if isinstance(n, int) and n == 0:
                e.wait_ge(sem("c_w_in"), 16 * 4)
            pe_transposes(xnc, banks(0, 2), np_, "c_tx")
            e.wait_ge(sem("c_xT"), (n + 1) * 2)
            need(e, "c_s", n)
            need(e, "c_free", (n - 1) * 32 + 4)
            for k in range(4):
                mm_sum(ps[0:np_, 2 + k, :], [(xTc[:, dc, 0:np_], wqs[:, dc, k * 512:(k + 1) * 512]) for dc in range(DC)],
                       "c_qmm")
                if k > 0:
                    q_transposes(e, n, k - 1)
            for k in range(4):
                if k == 2:
                    q_transposes(e, n, 3)
                e.wait_ge(sem("c_q"), n * 4 + k + 1)
                for c in range(4 * k, 4 * k + 4):
                    i = nc.tensor.matmul(ps[0:np_, 2 + k, (c % 4) * 128:(c % 4 + 1) * 128], qpT[:, c, 0:np_], kys[:, c, :],
                                         start=True, stop=True)
            i.then_inc(sem("c_smm"), 1)
            pe_transposes(xc, banks(0, 2), np_, "c_tx3")
        if t is not None:
            p = width(t)
            e.wait_ge(sem("c_sel"), t + 1)
            if n is not None:
                e.wait_ge(sem("c_x3T"), n + 1)
                e.wait_ge(sem("c_s"), n + 1)
            for k in range(3):
                i = nc.tensor.transpose(ps[:, 0, k * 128:k * 128 + p], sel[0:p, k, :], ident[0:p, 0:p])
            i.then_inc(sem("c_selt"), 1)
            with e.Fori(0, p // 16) as g:
                for u in range(4):
                    at_u = (t * 8 + g) * 4 + u + 1
                    e.wait_ge(sem("c_oneB"), at_u)
                    e.wait_ge(sem("c_gated"), at_u)
                    e.wait_ge(sem("c_free"), at_u)
                    for k in range(4):
                        i = nc.tensor.matmul(ps[:, G_BANK[u], k * 128:(k + 1) * 128], oneA[:, u, k, :], oneB[:, u, k, :],
                                             start=True, stop=True)
                    i.then_inc(sem("c_g"), 1)

    def c_act(e, t, n):
        if n is not None:
            np_ = width(n)
            for k in range(5):
                if k < 4:
                    e.wait_ge(sem("c_qmm"), n * 4 + k + 1)
                    need(e, "c_qt", n * 4 + k)
                    nc.scalar.activation(qtok[0:np_, :], ps[0:np_, 2 + k, :], ACT.Copy).then_inc(sem("c_qtok"), 1)
                if k > 0:
                    e.wait_ge(sem("c_qt"), n * 4 + k)
                    nc.scalar.activation(qpT[:, 4 * k - 4:4 * k, 0:np_],
                                         ps[:, 1 + k, :].rearrange("p (c t) -> p c t", c=4)[:, :, 0:np_], ACT.Copy).then_inc(sem("c_q"), 1)
        if t is not None:
            p = width(t)
            e.wait_ge(sem("c_cen"), t + 1)
            nc.scalar.activation(sel[0:p, 2, :], sel[0:p, 2, :], ACT.Exp).then_inc(sem("c_exp"), 1)
        if n is not None:
            e.wait_ge(sem("c_smm"), n + 1)
            nc.scalar.activation(skey[0:np_, :, :].rearrange("p a b -> p (a b)"), banks(2, 4)[0:np_, :], ACT.Copy).then_inc(sem("c_s"), 1)
            e.wait_ge(sem("c_tx3"), n + 1)
            need(e, "x3T_out", n * 16)
            nc.scalar.activation(x3T[:, :, 0:np_], banks(0, 2).rearrange("p (c t) -> p c t", c=DC)[:, :, 0:np_],
                                 ACT.Copy).then_inc(sem("c_x3T"), 1)
        if t is not None:
            need(e, "gates_out", t * 16)
            e.wait_ge(sem("c_selT"), t + 1)
            seen(e, "c_selT_seen_by_act")
            with e.Fori(0, p // 16) as g:
                for u in range(4):
                    e.wait_ge(sem("c_g"), (t * 8 + g) * 4 + u + 5)
                    nc.scalar.activation(gs[:, :, bass.ds(g * 16 + u * 4, 4)],
                                         ps[:, G_BANK[u], :].rearrange("p (t j) -> p j t", t=4), ACT.Copy).then_inc(sem("c_free"), 1)
        m = 0 if n is None and t is None else (None if n is None else n + 1)
        if m is not None and not (isinstance(m, int) and m > LAST):
            mp = width(m)
            e.wait_ge(sem("xc_in"), (m + 1) * 16)
            need(e, "c_rstd", m)
            nc.scalar.activation(banks(0, 2)[0:mp, :], xc[0:mp, :], ACT.Square,
                                 accum_out=ssq[0:mp, 0:1]).then_inc(sem("c_xssq"), 1)

    def took(p, s):
        out = pick[s][0:p, :].rearrange("p (c a) -> p c a", a=TOPK)
        iota16 = cst[0:p, C_IOTA:C_IOTA + TOPK].unsqueeze(1).to_broadcast([p, HK, TOPK])
        return out, iota16, wide(prow[0:p, s, :], TOPK)

    def keyed(p, s, keys):
        out = pick[s][0:p, :].rearrange("p (h k a) -> p h k a", h=PH, k=TOPK)
        return out, out, keys.unsqueeze(2).to_broadcast([p, PH, TOPK, TOPK])

    def c_pool(e, ch, t, n):
        if t is not None:
            p = width(t)
            e.wait_ge(sem("c_took"), t + 1)
            nc.gpsimd.tensor_tensor(*keyed(p, 1, i16f[0:p, :, :]), ALU.mult).then_inc(sem("c_picked"), 1)
            with e.Fori(0, p // 16) as g:
                for u in range(4):
                    e.wait_ge(sem("c_oneA"), (t * 8 + g) * 4 + u + 1)
                    nc.gpsimd.tensor_tensor(oneA[:, u, :, :], oneA[:, u, :, :], wide(selT[:, 2, bass.ds(g * 16 + u * 4, 4)], 128),
                                            ALU.mult).then_inc(sem("c_gated"), 1)
        m = 0 if n is None and t is None else (None if n is None else n + 1)
        if m is not None and not (isinstance(m, int) and m > LAST):
            mp = width(m)
            e.wait_ge(sem("c_xssq"), m + 1)
            need(e, "c_xn", m)
            seen(e, "c_xssq_seen")
            rsqrt_mean(ch, ssq[0:mp, 0:1], rst[0:mp, 0:1], 1.0 / D, mp, 0, 1).then_inc(sem("c_rstd"), 1)

    def top16(ch, out16, idx16, vals, cnt, between=None):
        for k in range(cnt):
            nc.vector.max(out16[:, k, 0:8], vals[:, k, :])
        if between:
            between()
        ch.wait()
        for k in range(cnt):
            nc.vector.max_index(idx16[:, k, 0:8], out16[:, k, 0:8], vals[:, k, :])
        ch.wait()
        for k in range(cnt):
            nc.vector.match_replace(out=vals[:, k, :], in_to_replace=out16[:, k, 0:8], in_values=vals[:, k, :], imm_value=GONE)
        ch.wait()
        for k in range(cnt):
            nc.vector.max(out16[:, k, 8:16], vals[:, k, :])
        ch.wait()
        for k in range(cnt):
            nc.vector.max_index(idx16[:, k, 8:16], out16[:, k, 8:16], vals[:, k, :])

    def c_dve(e, ch, t, n):
        if n is not None:
            np_ = width(n)
            e.wait_ge(sem("c_rstd"), n + 1)
            need(e, "c_tx", n)
            nc.vector.tensor_scalar(xnc[0:np_, :], xc[0:np_, :], rst[0:np_, 0:1], None, ALU.mult).then_inc(sem("c_xn"), 1)

        def xT_out():
            e.wait_ge(sem("c_tx"), n + 1)
            need(e, "xnT_out", n * 16)
            need(e, "c_qmm", n * 4)
            for k in range(2):
                gained(xTc, banks(0, 2), 4, np_, k * 4, 4).then_inc(sem("c_xT"), 1)

        if t is None:
            xT_out()
        else:
            p = width(t)
            e.wait_ge(sem("c_s"), t + 1)
            e.wait_ge(sem("c_g"), t * 32 + 4)
            seen(e, "c_s_seen")
            top16(ch, v16[0:p], i16[0:p], skey[0:p], 2 * PH, xT_out if n is not None else None)
            v16v = v16[0:p, :, :].rearrange("p (h s) k -> p h s k", s=2)
            i16v = i16[0:p, :, :].rearrange("p (h s) k -> p h s k", s=2)
            nc.vector.tensor_tensor(cand[0:p, :, :].rearrange("p h (a b) -> p h a b", a=TOPK), wide(v16v[:, :, 0, :], TOPK),
                                    v16v[:, :, 1, :].unsqueeze(2).to_broadcast([p, PH, TOPK, TOPK]), ALU.add)
            ch.wait()
            top16(ch, top[0:p], pos[0:p], cand[0:p], PH)
            ch.wait()
            g2 = sel[0:p, 2, :].rearrange("p (h k) -> p h k", h=PH)
            nc.vector.tensor_tensor(g2, top[0:p, :, :], top[0:p, :, 0:1].to_broadcast([p, PH, TOPK]), ALU.subtract).then_inc(sem("c_cen"), 1)
            posf = pos[0:p, :, :].rearrange("p a b -> p (a b)")
            nc.vector.tensor_scalar(prow[0:p, 0, :], posf, 4, None, ALU.logical_shift_right)
            nc.vector.tensor_copy(i16f[0:p, :, :], i16v[:, :, 1, :])
            ch(nc.vector.tensor_scalar(prow[0:p, 1, :], posf, 15, None, ALU.bitwise_and))
            nc.vector.tensor_tensor(*took(p, 1), ALU.is_equal).then_inc(sem("c_took"), 1)
            ch(nc.vector.tensor_tensor(*took(p, 0), ALU.is_equal))
            ch(nc.vector.tensor_tensor(*keyed(p, 0, i16v[:, :, 0, :]), ALU.mult))
            ch(nc.vector.tensor_reduce(sel[0:p, 0, :], took(p, 0)[0], AX.X, ALU.add))
            e.wait_ge(sem("c_exp"), t + 1)
            ch(nc.vector.tensor_reduce(gsum[0:p, 0, :], g2, AX.X, ALU.add))
            ch(nc.vector.reciprocal(gsum[0:p, 1, :], gsum[0:p, 0, :]))
            nc.vector.tensor_tensor(g2, g2, wide(gsum[0:p, 1, :], TOPK), ALU.mult)
            e.wait_ge(sem("c_picked"), t + 1)
            ch(nc.vector.tensor_reduce(sel[0:p, 1, :], took(p, 1)[0], AX.X, ALU.add))
            e.sem_inc(sem("c_sel"), 1)
            e.wait_ge(sem("c_selt"), t + 1)
            nc.vector.tensor_copy(selT[:, :, 0:p], ps[:, 0, 0:384].rearrange("p (a b) -> p a b", a=3)[:, :, 0:p]).then_inc(sem("c_selT"), 1)
            e.wait_ge(sem("c_selT"), t + 1)
            seen(e, "c_selT_seen_by_dve")
            with e.Fori(0, p // 16) as g:
                iota = cst[:, C_IOTA:C_IOTA + 128].unsqueeze(1).to_broadcast([128, 4, 128])
                for u in range(4):
                    e.wait_ge(sem("c_g"), (t * 8 + g) * 4 + u + 1)
                    nc.vector.tensor_tensor(oneA[:, u, :, :], iota, wide(selT[:, 0, bass.ds(g * 16 + u * 4, 4)], 128),
                                            ALU.is_equal).then_inc(sem("c_oneA"), 1)
                    nc.vector.tensor_tensor(oneB[:, u, :, :], iota, wide(selT[:, 1, bass.ds(g * 16 + u * 4, 4)], 128),
                                            ALU.is_equal).then_inc(sem("c_oneB"), 1)


    def group(k):
        o, w = TG[k % len(TG)]
        return k // len(TG), o, w, ps[:, V_BANKS[k % len(V_BANKS)], 0:w]

    def last_group_on(b):
        return max(k for k in range(NGRP) if V_BANKS[k % len(V_BANKS)] == b)

    def d_hidden(e, p):
        e.wait_ge(sem("u_hi"), p + 1)
        e.wait_ge(sem("u_lo"), p + 1)
        for j in range(2):
            for k, (o, w) in enumerate(TG):
                need(e, "gelu", (p - 1) * 6 + j * 3 + k + 1 if not known(p, 0) else 0)
                if j == 0 and not (isinstance(p, int) and p < 2):
                    e.wait_ge(sem("added"), (p - 2) * NGRP + last_group_on(H_BANKS[0][k]) + 1)
                parts = [(a[:, j, dc * 128:(dc + 1) * 128], b[:, dc, o:o + w])
                         for dc in range(DC) for a, b in ((uh, xh), (uh, xl), (ul, xh))]
                mm_sum(ps[:, H_BANKS[j][k], 0:w], parts, "hidden")

    def d_output(e, p, par):
        e.wait_ge(sem("v_lo"), p + 1)
        e.wait_ge(sem("w_lo"), p * 2 + 2)
        for k in range(NGRP):
            dc, o, w, out = group(k)
            b = V_BANKS[k % len(V_BANKS)]
            if k >= len(V_BANKS):
                e.wait_ge(sem("added"), p * NGRP + k - len(V_BANKS) + 1)
            elif b in H_BANKS[0] and not known(p, NPAIR - 1):
                e.wait_ge(sem("gelu"), (p + 1) * 6 + b + 1)
            else:
                need(e, "added", (p - 1) * NGRP + last_group_on(b) + 1 if not known(p, 0) else 0)
            parts = [(a[:, j, dc * 128:(dc + 1) * 128], x_[:, j, o:o + w])
                     for j in range(2) for a, x_ in ((vh, wh[par]), (vh, wl[par]), (vl, wh[par]))]
            mm_sum(out, parts, "output")

    def d_pe(e):
        e.wait_ge(sem("xl_ready"), 4)
        d_hidden(e, 0)
        for p in (0, 1):
            d_hidden(e, p + 1)
            d_output(e, p, p)
        with e.Fori(2, NPAIR - 2, 2) as p:
            for q in range(2):
                d_hidden(e, p + q + 1)
                d_output(e, p + q, q)
        d_hidden(e, NPAIR - 1)
        d_output(e, NPAIR - 2, 0)
        d_output(e, NPAIR - 1, 1)
        for t in range(NT + 1):
            p = width(t)
            e.wait_ge(sem("added"), NPAIR * NGRP)
            if t >= 4:
                e.wait_ge(sem("y_scaled"), t - 3)
            for dc in range(DC):
                i = nc.tensor.transpose(banks(2 * (t % 4), 2)[0:p, dc * 128:(dc + 1) * 128], acc[:, dc, t * 128:t * 128 + p], ident)
            i.then_inc(sem("y_t"), 1)

    def d_split_u(e, p):
        e.wait_ge(sem("u_in"), (p + 1) * 16)
        need(e, "hidden", p * 6)
        nc.scalar.activation(uh[:], ur[:], ACT.Copy).then_inc(sem("u_hi"), 1)

    def d_split_v(e, p):
        e.wait_ge(sem("v_in"), (p + 1) * 16)
        need(e, "output", p * NGRP)
        nc.scalar.activation(vh[:], vr[:], ACT.Copy).then_inc(sem("v_hi"), 1)

    def d_gelu(e, p, par):
        for j in range(2):
            need(e, "w_lo", (p - 1) * 2 + j + 1 if not known(p, 0) else 0)
            for k, (o, w) in enumerate(TG):
                e.wait_ge(sem("hidden"), p * 6 + j * 3 + k + 1)
                nc.scalar.activation(hid[:, j, o:o + w], ps[:, H_BANKS[j][k], 0:w], ACT.Gelu_apprx_tanh).then_inc(sem("gelu"), 1)
            e.wait_ge(sem("gated"), p * 2 + j + 1)
            nc.scalar.activation(wh[par][:, j, :], hid[:, j, :], ACT.Copy).then_inc(sem("w_hi"), 1)

    def d_act(e):
        e.wait_ge(sem("xf_in"), 16)
        e.wait_ge(sem("c_g"), NT * 32 + SAMPLE // 4 + 4)
        d_split_u(e, 0)
        for k in range(4):
            c = slice(2 * k, 2 * k + 2)
            nc.scalar.activation(xh[:, c, :], xf[:, c, :], ACT.Copy).then_inc(sem("xh_ready"), 1)
        e.wait_ge(sem("xl_ready"), 4)
        d_split_u(e, 1)
        e.wait_ge(sem("gates_out"), (NT + 1) * 16)
        d_gelu(e, 0, 0)
        for p in (0, 1):
            d_split_v(e, p)
            d_gelu(e, p + 1, 1 - p)
            d_split_u(e, p + 2)
        with e.Fori(2, NPAIR - 2, 2) as p:
            for q in range(2):
                d_split_v(e, p + q)
                d_gelu(e, p + q + 1, 1 - q)
                d_split_u(e, p + q + 2)
        d_split_v(e, NPAIR - 2)
        d_gelu(e, NPAIR - 1, 1)
        d_split_v(e, NPAIR - 1)
        for t in range(NT + 1):
            p = width(t)
            e.wait_ge(sem("y_t"), t + 1)
            need(e, "y_rstd", t)
            nc.scalar.activation(ysq[0:p, :], banks(2 * (t % 4), 2)[0:p, :], ACT.Square, accum_out=ssq[0:p, 0:1]).then_inc(sem("y_ssq"), 1)

    def d_pool(e, ch):
        for t in range(NT + 1):
            p = width(t)
            e.wait_ge(sem("y_ssq"), t + 1)
            need(e, "y_scaled", t)
            rsqrt_mean(ch, ssq[0:p, 0:1], rst[0:p, 0:1], 1.0 / D, p, 0, 1).then_inc(sem("y_rstd"), 1)

    def d_low_u(e, p):
        e.wait_ge(sem("u_hi"), p + 1)
        nc.vector.tensor_tensor(ul[:], ur[:], uh[:].bitcast(F32), ALU.subtract).then_inc(sem("u_lo"), 1)

    def d_low_v(e, p):
        e.wait_ge(sem("v_hi"), p + 1)
        nc.vector.tensor_tensor(vl[:], vr[:], vh[:].bitcast(F32), ALU.subtract).then_inc(sem("v_lo"), 1)

    def d_gate(e, p, par):
        for j in range(2):
            e.wait_ge(sem("g_in"), (p + 1) * 16)
            e.wait_ge(sem("gelu"), p * 6 + j * 3 + 3)
            nc.vector.tensor_tensor(hid[:, j, :], hid[:, j, :], gp[:, j, :], ALU.mult).then_inc(sem("gated"), 1)
            e.wait_ge(sem("w_hi"), p * 2 + j + 1)
            need(e, "output", (p - 1) * NGRP if not known(p, 0) else 0)
            nc.vector.tensor_tensor(wl[par][:, j, :], hid[:, j, :], wh[par][:, j, :].bitcast(F32), ALU.subtract).then_inc(sem("w_lo"), 1)

    def d_add(e, p, a, b):
        for k in range(a, b):
            dc, o, w, out = group(k)
            e.wait_ge(sem("output"), p * NGRP + k + 1)
            nc.vector.tensor_tensor(acc[:, dc, o:o + w], acc[:, dc, o:o + w], out, ALU.add).then_inc(sem("added"), 1)

    def d_dve(e):
        d_low_u(e, 0)
        for k in range(4):
            c = slice(2 * k, 2 * k + 2)
            e.wait_ge(sem("xh_ready"), k + 1)
            nc.vector.tensor_tensor(xl[:, c, :], xf[:, c, :], xh[:, c, :].bitcast(F32), ALU.subtract).then_inc(sem("xl_ready"), 1)
        d_low_u(e, 1)
        d_gate(e, 0, 0)
        e.wait_ge(sem("acc_in"), 16)

        def step(p, par):
            d_low_v(e, p)
            d_gate(e, p + 1, 1 - par)
            d_add(e, p, 0, 8)
            if not known(p, NPAIR - 2):
                d_low_u(e, p + 2)
            d_add(e, p, 8, NGRP)

        step(0, 0)
        step(1, 1)
        with e.Fori(2, NPAIR - 2, 2) as p:
            step(p, 0)
            step(p + 1, 1)
        step(NPAIR - 2, 0)
        d_low_v(e, NPAIR - 1)
        d_add(e, NPAIR - 1, 0, NGRP)
        e.wait_ge(sem("final_gain_in"), 16)
        for t in range(NT + 1):
            p = width(t)
            e.wait_ge(sem("y_rstd"), t + 1)
            if t >= 2:
                e.wait_ge(sem(f"y_out_{t % 2}"), t // 2 * 16)
            nc.vector.scalar_tensor_tensor(yo[0:p, t % 2, :], banks(2 * (t % 4), 2)[0:p, :], rst[0:p, 0:1], fgain[0:p, :],
                                           op0=ALU.mult, op1=ALU.mult).then_inc(sem("y_scaled"), 1)

    with nc.Block() as block:
        @block.gpsimd
        def _(pool):
            ch = Chain(pool, "pool_step")
            pool.wait_ge(sem("half_ready"), 1)
            a_pool(pool, ch, None, None)
            a_pool(pool, ch, None, 0)
            a_pool(pool, ch, 0, 1)
            with pool.Fori(1, NT - 2) as t:
                ch.enter(t, 1, 3)
                a_pool(pool, ch, t, t + 1)
                ch.leave(NT - 2)
            a_pool(pool, ch, NT - 2, NT - 1)
            a_pool(pool, ch, NT - 1, NT)
            a_pool(pool, ch, NT, None)
            for m in range(2):
                m_pool(pool, ch, m)
            pool.wait_ge(sem("m_xn"), 2)
            b_pool(pool, ch, None, None)
            b_pool(pool, ch, None, 0)
            b_pool(pool, ch, 0, 1)
            with pool.Fori(1, NT - 2) as t:
                ch.enter(t, 1, 1)
                b_pool(pool, ch, t, t + 1)
                ch.leave(NT - 2)
            b_pool(pool, ch, NT - 2, NT - 1)
            c_pool(pool, ch, None, None)
            c_pool(pool, ch, None, 0)
            c_pool(pool, ch, 0, 1)
            with pool.Fori(1, NT - 2) as t:
                ch.enter(t, 1, 1)
                c_pool(pool, ch, t, t + 1)
                ch.leave(NT - 2)
            c_pool(pool, ch, NT - 2, NT - 1)
            c_pool(pool, ch, NT - 1, NT)
            c_pool(pool, ch, NT, None)
            d_pool(pool, ch)

        @block.scalar
        def _(act):
            a_act(act, None, None)
            a_act(act, None, 0)
            a_act(act, 0, 1)
            with act.Fori(1, NT - 2) as t:
                a_act(act, t, t + 1)
            a_act(act, NT - 2, NT - 1)
            a_act(act, NT - 1, NT)
            a_act(act, NT, None)
            for m in range(2):
                m_act(act, m)
            act.wait_ge(sem("m_rstd"), 2)
            b_act(act, None, None)
            b_act(act, None, 0)
            b_act(act, 0, 1)
            with act.Fori(1, NT - 2) as t:
                b_act(act, t, t + 1)
            b_act(act, NT - 2, NT - 1)
            b_act(act, NT - 1, NT)
            b_act(act, NT, None)
            act.sem_inc(sem("c_free"), 4)
            c_act(act, None, None)
            c_act(act, None, 0)
            c_act(act, 0, 1)
            with act.Fori(1, NT - 2) as t:
                c_act(act, t, t + 1)
            c_act(act, NT - 2, NT - 1)
            c_act(act, NT - 1, NT)
            c_act(act, NT, None)
            d_act(act)

        @block.vector
        def _(dve):
            ch = Drained(dve)
            setup_dve(dve)
            a_dve(dve, ch, None, 0)
            ws_dve(dve)
            a_dve(dve, ch, 0, 1)
            with dve.Fori(1, NT - 2) as t:
                a_dve(dve, ch, t, t + 1)
            a_dve(dve, ch, NT - 2, NT - 1)
            a_dve(dve, ch, NT - 1, NT)
            s_bias_dve(dve)
            a_dve(dve, ch, NT, None)
            a_dve_tail(dve)
            for m in range(2):
                m_dve(dve, m)
            dve.wait_ge(sem("m_mm"), 4)
            b_dve(dve, ch, None, 0)
            b_dve(dve, ch, 0, 1)
            with dve.Fori(1, NT - 2) as t:
                b_dve(dve, ch, t, t + 1)
            b_dve(dve, ch, NT - 2, NT - 1)
            b_dve(dve, ch, NT - 1, NT)
            b_dve(dve, ch, NT, None)
            c_dve(dve, ch, None, 0)
            c_dve(dve, ch, 0, 1)
            with dve.Fori(1, NT - 2) as t:
                c_dve(dve, ch, t, t + 1)
            c_dve(dve, ch, NT - 2, NT - 1)
            c_dve(dve, ch, NT - 1, NT)
            c_dve(dve, ch, NT, None)
            d_dve(dve)

        @block.tensor
        def _(pe):
            setup_pe(pe)
            a_pe(pe, None, 0)
            a_pe(pe, 0, 1)
            with pe.Fori(1, NT - 1) as t:
                a_pe(pe, t, t + 1)
            a_pe(pe, NT - 1, NT)
            s_bias_pe(pe)
            a_pe(pe, NT, None)
            a_pe_tail(pe)
            for m in range(2):
                m_pe(pe, m)
            b_pe(pe, None, 0)
            b_pe(pe, 0, 1)
            with pe.Fori(1, NT - 1) as t:
                b_pe(pe, t, t + 1)
            b_pe(pe, NT - 1, NT)
            b_pe(pe, NT, None)
            pe.sem_inc(sem("c_g"), 4)
            c_pe(pe, None, 0)
            c_pe(pe, 0, 1)
            with pe.Fori(1, NT - 1) as t:
                c_pe(pe, t, t + 1)
            c_pe(pe, NT - 1, NT)
            c_pe(pe, NT, None)
            d_pe(pe)

        @block.sync
        def _(sp):
            def load(dst, src, name):
                sp.dma_start(dst, src).then_inc(sem(name), 16)

            load(xres[:, 0, :], x[0:128, :], "x_in_0")
            load(cst[:], consts, "const_in")
            load(gain[:], gains, "const_in")
            load(sink[:], sinks.partition_broadcast(128), "const_in")
            load(relS[:], rel, "const_in")
            load(lnrow[:], rows[0:2, :].partition_broadcast(128), "const_in")
            load(sbs[:], sbias, "const_in")
            load(sbsS[:], sbiasS, "const_in")
            sp.wait_ge(sem("toep_sb"), 1)
            load(toep_d, toepS, "toep_moved")
            sp.wait_ge(sem("toep_moved"), 16)
            load(hank[:], bass.AP(toep_d.tensor, 0, [[1, 128], [TOEP, NH], [1, 2 * WIN]]), "toep_moved")
            load(win[:], w_in, "w_in_in")
            load(wsTs[:], wsT, "tokens_ws_in")
            load(wsSs[:], wsS, "tokens_ws_in")
            load(xres[:, 1:NT, :], x[128:SEQ, :].rearrange("(t p) d -> p t d", p=128), "tokens_ws_in")
            load(xres[0:SAMPLE, NT, :], x[SEQ:T, :], "tokens_ws_in")
            load(wout[:], w_out, "w_out_in")
            load(swa_ks[:, 0:WIN - DEC_L, :], swa_k_old[:, DEC_L:WIN, :], "swa_old_out")
            load(swa_vs[:, 0:WIN - DEC_L, :], swa_v_old[:, DEC_L:WIN, :], "swa_old_out")
            sp.wait_ge(sem("a_kvsb"), (NT + 1) * 2)
            load(swa_vs[:, WIN - DEC_L:WIN, :].rearrange("b l c -> b l c"), kv[0:SAMPLE, NT, KV:2 * KV], "v_new_out")
            load(swa_ks[:, WIN - DEC_L:WIN, :], kv[0:SAMPLE, NT, 0:KV], "kv_out")
            load(swa_kp, kv[:, NT - 1, 0:KV], "kv_out")
            load(swa_vp, kv[:, NT - 1, KV:2 * KV], "kv_out")
            sp.wait_ge(sem("a_qmm"), NT + 1)
            load(wmk[:], w_mk, "m_w_in")
            load(wmv[:], w_mv, "m_w_in")
            load(kTc_s[:], kTc, "s_in")
            load(vc_s[:], vc, "s_in")
            sp.wait_ge(sem("v_new_out"), 16)
            load(vnew[:], swa_vs[:, WIN - DEC_L:WIN, :].rearrange("b l c -> l b c"), "s_vnew")
            sp.wait_ge(sem("a_vln"), NT + 1)
            load(chunk_v, vln[0:SAMPLE, :], "kv_out")
            sp.wait_ge(sem("swa_old_out"), 32)
            sp.wait_ge(sem("kv_out"), 64)
            sp.wait_ge(sem("a_xmid"), (NT + 1) * 2)
            load(memx, mem[0:128, :], "mem_in")
            load(wmq[:], w_mq, "b_w_in")
            load(wmo[:], w_mo, "b_w_in")
            sp.wait_ge(sem("m_xn"), 1)
            load(memx, mem[128:256, :], "mem_in")
            load(mkTc_s[:], mkTc, "b_cache_in")
            load(mvc_s[:], mvc, "b_cache_in")
            sp.wait_ge(sem("m_kv"), 4)
            load(mem_k.rearrange("(m p) c -> p m c", p=128), mkv[:, :, 0, :], "mem_out")
            load(mem_v.rearrange("(m p) c -> p m c", p=128), mkv[:, :, 1, :], "mem_out")
            sp.wait_ge(sem("m_mm"), 4)
            load(wqs[:, 0:4, :], wq[:, 0:4, :], "c_w_in")
            for t in range(NT + 1):
                if t == NT:
                    sp.wait_ge(sem("b_qmm"), NT + 1)
                    load(wqs[:, 4:6, :], wq[:, 4:6, :], "c_w_in")
                sp.wait_ge(sem("b_xmid"), (t + 1) * 2)
                load(x3_d[t * 128:t * 128 + width(t), :], xres[0:width(t), t, :], "x3_out")
            sp.wait_ge(sem("b_out"), (NT + 1) * 2)
            load(wqs[:, 6:8, :], wq[:, 6:8, :], "c_w_in")
            sp.wait_ge(sem("mem_out"), 32)
            sp.wait_ge(sem("x3_out"), (NT + 1) * 16)
            load(xc[:], x3_d[0:128, :], "xc_in")
            load(kys[:], keysT, "c_w_in")

            def tiles_in_out(n):
                w = width(n)
                cols = bass.ds(n * 128, w)
                sp.wait_ge(sem("c_xT"), (n + 1) * 2)
                load(xnT_d[:, :, cols], xTc[:, :, 0:w], "xnT_out")
                sp.wait_ge(sem("c_x3T"), n + 1)
                load(x3T_d[:, :, cols], x3T[:, :, 0:w], "x3T_out")

            def next_in(n):
                sp.wait_ge(sem("c_xn"), n)
                sp.wait_ge(sem("c_tx3"), n)
                load(xc[0:width(n), :], x3_d[bass.ds(n * 128, width(n)), :], "xc_in")

            def gates_to_dram(t, quads):
                sp.wait_ge(sem("c_free"), quads + 4)
                load(gates_d[:, :, bass.ds(t * 128, width(t))], gs[:, :, 0:width(t)], "gates_out")

            tiles_in_out(0)
            next_in(1)
            tiles_in_out(1)
            next_in(2)
            gates_to_dram(0, 32)
            with sp.Fori(1, NT - 2) as t:
                tiles_in_out(t + 1)
                next_in(t + 2)
                gates_to_dram(t, (t + 1) * 32)
            tiles_in_out(NT - 1)
            next_in(NT)
            gates_to_dram(NT - 2, (NT - 1) * 32)
            tiles_in_out(NT)
            sp.wait_ge(sem("x3T_out"), (NT + 1) * 16)
            sp.wait_ge(sem("xnT_out"), (NT + 1) * 16)
            sp.wait_ge(sem("c_qmm"), (NT + 1) * 4)
            load(xf[:], xnT_d, "xf_in")
            load(ur[:], u_t[:, 0:2, :], "u_in")
            load(vr[:], v_w[:, 0:2, :], "v_in")
            gates_to_dram(NT - 1, NT * 32)
            gates_to_dram(NT, NT * 32 + SAMPLE // 4)
            sp.wait_ge(sem("u_lo"), 1)
            load(ur[:], u_t[:, 2:4, :], "u_in")
            sp.wait_ge(sem("gates_out"), (NT + 1) * 16)
            load(gp[:], gates_d[:, 0:2, :], "g_in")
            load(acc[:], x3T_d, "acc_in")
            sp.wait_ge(sem("gated"), 2)
            load(gp[:], gates_d[:, 2:4, :], "g_in")
            sp.wait_ge(sem("v_lo"), 1)
            load(vr[:], v_w[:, 2:4, :], "v_in")
            with sp.Fori(2, NPAIR) as p:
                sp.wait_ge(sem("u_lo"), p)
                load(ur[:], u_t[:, bass.ds(p * 2, 2), :], "u_in")
                sp.wait_ge(sem("gated"), p * 2)
                load(gp[:], gates_d[:, bass.ds(p * 2, 2), :], "g_in")
                sp.wait_ge(sem("v_lo"), p)
                load(vr[:], v_w[:, bass.ds(p * 2, 2), :], "v_in")
            sp.wait_ge(sem("v_lo"), NPAIR)
            load(fgain[:], final.partition_broadcast(128), "final_gain_in")
            for t in range(NT + 1):
                sp.wait_ge(sem("y_scaled"), t + 1)
                load(y[t * 128:t * 128 + width(t), :], yo[0:width(t), t % 2, :], f"y_out_{t % 2}")
            sp.wait_ge(sem("y_out_0"), (NT // 2 + 1) * 16)
            sp.wait_ge(sem("y_out_1"), NT // 2 * 16)
            for name in SEEN:
                sp.wait_ge(sem(name), NT + 1)


def bucket_constants():
    c = np.zeros((128, C_W), np.float32)
    i = np.arange(128)
    c[:, C_ID:C_ID + 128] = np.eye(128)
    c[:, C_FLIP:C_FLIP + 128] = np.eye(128)[::-1]
    c[:, C_TRIL:C_TRIL + 128] = i[:, None] <= i[None, :]
    s = np.arange(SAMPLE)
    c[:SAMPLE, C_BD:C_BD + SAMPLE] = (s[:, None] // DEC_L == s[None, :] // DEC_L) & (s[:, None] <= s[None, :])
    c[:, C_IOTA:C_IOTA + 128] = i
    exact = BUCKETS // 2
    for m in range(TOEP):
        d = 2 * WIN - 1 - m
        if 0 <= d < WIN:
            large = exact + int(np.float32(np.log(np.float32(max(d, 1)) / np.float32(exact)))
                                / np.float32(np.log(WIN / exact)) * np.float32(BUCKETS - exact))
            c[d if d < exact else min(large, BUCKETS - 1), C_OH + m] = 1.0
        else:
            c[:NH, C_MASK + m] = NEG
    c[:DEC_L, C_ROW:C_ROW + SAMPLE] = np.arange(DEC_L)[:, None] == s[None, :] % DEC_L
    return c


def chunked(w):
    return np.ascontiguousarray(w.reshape(-1, 128, w.shape[-1]).transpose(1, 0, 2))


def by_chunk(v):
    return v.reshape(-1, 128).T


def laid_out(inp):
    a = {k: np.asarray(v) for k, v in inp.items()}
    l0 = {k: v[0] for k, v in a.items()}
    w = a["w_in"][0]
    q = w[:, Q0:K0].reshape(D, NKV, 4, HD).transpose(0, 2, 1, 3).reshape(D, NH * HD)
    gains = np.zeros((128, 6, DC), np.float32)
    gains[:, 0] = by_chunk(l0["norm_mix_g"])
    gains[:, 1] = by_chunk(np.concatenate([l0["norm_a_out_g"], l0["norm_b_out_g"]]))
    gains[:, 2] = by_chunk(l0["norm_mem_g"])
    gains[:, 3] = by_chunk(l0["norm_memsrc_g"])
    gains[:, 4] = by_chunk(l0["norm_ffn_g"])
    wsT = l0["spatial_w"].transpose(2, 0, 1)
    r = lambda k: l0[k].reshape(DEC_B, WIN, KV)
    return dict(
        x=np.concatenate([a["x_prompt"].reshape(SEQ, D), a["x_sample"].reshape(SAMPLE, D)]),
        mem=a["mem_prompt"].reshape(NMEM, D),
        kTc=r("cache_swa_k").transpose(2, 0, 1), vc=r("cache_swa_v").transpose(1, 0, 2),
        mkTc=l0["cache_mem_k"].transpose(3, 0, 2, 1),
        mvc=l0["cache_mem_v"].reshape(DEC_B, 2, 128, MW).transpose(2, 0, 1, 3),
        swa_k_old=r("cache_swa_k"), swa_v_old=r("cache_swa_v"),
        gains=gains, rows=np.stack([l0["ln_v_g"], l0["ln_v_b"]]), final=a["norm_final_g"].reshape(1, D),
        w_in=chunked(np.concatenate([w[:, :Q0], q, w[:, K0:]], axis=1)), w_out=chunked(l0["w_out"]),
        wsT=wsT, wsS=np.tile(wsT[:DEC_L, :, :DEC_L], (DEC_B, 1, DEC_B)),
        sbias=l0["spatial_b"].T, sbiasS=np.tile(l0["spatial_b"].T[:DEC_L], (DEC_B, 1)),
        rel=a["rel_bias"], sinks=a["attn_sinks"].reshape(1, NH),
        w_mq=chunked(l0["w_mq"]), w_mk=chunked(l0["w_mk"]), w_mv=chunked(l0["w_mv"]), w_mo=chunked(l0["w_mo"]),
        wq=chunked(l0["peer_wq"]), keysT=l0["peer_keys"].reshape(2 * PH, PK, 128).transpose(2, 0, 1),
        u_t=l0["peer_u"].reshape(PK, PK, DC, 128).transpose(3, 1, 2, 0).reshape(128, PK, D),
        v_w=l0["peer_v"].reshape(PK, PK, D), consts=bucket_constants())


OUTS = dict(y=(T, D), swa_kp=(WIN, KV), swa_vp=(WIN, KV), mem_k=(NMEM, MW), mem_v=(NMEM, MW),
            swa_ks=(DEC_B, WIN, KV), swa_vs=(DEC_B, WIN, KV), chunk_v=(SAMPLE, MIXC))


def kernel(**inputs):
    import concourse.bacc as bacc
    from concourse.bass_utils import run_bass_kernel_spmd

    nc = bacc.Bacc("TRN2", target_bir_lowering=False, num_devices=1)
    arrays = {k: np.ascontiguousarray(v) for k, v in laid_out(inputs).items()}
    args = {k: nc.dram_tensor(k, v.shape, mybir.dt.from_np(v.dtype), kind="ExternalInput").ap() for k, v in arrays.items()}
    outs = {k: nc.dram_tensor("out_" + k, s, F32, kind="ExternalOutput").ap() for k, s in OUTS.items()}
    hymba_step_kernel(nc, **args, **outs)
    r = run_bass_kernel_spmd(nc, [arrays], core_ids=[0]).results[0]
    o = {k: r["out_" + k] for k in OUTS}
    return (o["y"][:SEQ].reshape(1, SEQ, D), o["y"][SEQ:].reshape(DEC_B, DEC_L, D),
            o["swa_kp"].reshape(1, 1, WIN, NKV, HD), o["swa_vp"].reshape(1, 1, WIN, NKV, HD),
            o["mem_k"].reshape(1, 1, NMEM, MH, MD), o["mem_v"].reshape(1, 1, NMEM, MH, MD),
            o["swa_ks"].reshape(1, DEC_B, WIN, NKV, HD), o["swa_vs"].reshape(1, DEC_B, WIN, NKV, HD),
            o["chunk_v"].reshape(1, DEC_B, DEC_L, GRP, MIXC // GRP))
```
